# Optimizing a Trainium2 kernel written in Bass

```python
import jax, jax.numpy as jnp
from jax import lax
import numpy as np

D_MODEL = 1024
BATCH = 1
SEQ = 256
DEPTH = 2

HEAD_DIM = 64
MLA_HEADS = 8
MLA_Q_RANK = 192
MLA_KV_RANK = 128
MLA_NOPE = 64
MLA_ROPE = 32
MLA_V = 64
ROPE_THETA = 10000.0
FOX_HEADS = 8
DSA_HEADS = 8
IDX_HEADS = 8
IDX_DIM = 32
DSA_MAX_TOPK = 256
N_BRANCH = 3
BRANCH_WIDTH = MLA_HEADS * MLA_V
D_FF = 2816
CONV_WIDTH = 3
Q_BLOCK = 128
LN_EPS = 1e-5
RMS_EPS = 1e-6
DEEPNORM_ALPHA = (2 * DEPTH) ** 0.25
DEEPNORM_BETA = (8 * DEPTH) ** -0.25

SPLIT_SIZES = (
    MLA_Q_RANK, MLA_KV_RANK, MLA_ROPE,
    FOX_HEADS * HEAD_DIM, FOX_HEADS * HEAD_DIM, FOX_HEADS * HEAD_DIM, FOX_HEADS,
    DSA_HEADS * HEAD_DIM, HEAD_DIM, HEAD_DIM,
    IDX_HEADS * IDX_DIM, IDX_DIM, IDX_HEADS,
    N_BRANCH * D_MODEL,
)
D_IN = sum(SPLIT_SIZES)

kernel_name = 'hybrid_mla_fox_dsa_deepnorm'

def _layernorm(x, g, b):
    xf = x.astype(jnp.float32)
    mu = jnp.mean(xf, -1, keepdims=True)
    var = jnp.mean(jnp.square(xf - mu), -1, keepdims=True)
    return ((xf - mu) * lax.rsqrt(var + LN_EPS) * g + b).astype(x.dtype)

def _rmsnorm(x, g):
    xf = x.astype(jnp.float32)
    return (xf * lax.rsqrt(jnp.mean(jnp.square(xf), -1, keepdims=True) + RMS_EPS) * g).astype(x.dtype)

def _split_cols(z):
    parts = []
    off = 0
    for width in SPLIT_SIZES:
        parts.append(z[..., off:off + width])
        off += width
    return parts

def _rope(x, pos):
    half = x.shape[-1] // 2
    inv = ROPE_THETA ** (-jnp.arange(half, dtype=jnp.float32) / half)
    ang = pos.astype(jnp.float32)[..., None] * inv
    cos = jnp.cos(ang)[:, :, None, :]
    sin = jnp.sin(ang)[:, :, None, :]
    xf = x.astype(jnp.float32)
    x1, x2 = xf[..., :half], xf[..., half:]
    return jnp.concatenate([x1 * cos - x2 * sin, x1 * sin + x2 * cos], -1).astype(x.dtype)

def _alibi_slopes(n):
    return jnp.exp2(-8.0 * jnp.arange(1, n + 1, dtype=jnp.float32) / n)

def _sweep_blocks(block_fn, seq):
    starts = jnp.arange(seq // Q_BLOCK, dtype=jnp.int32) * Q_BLOCK
    out = lax.map(block_fn, starts)
    nb, b, qb, h, dv = out.shape
    return jnp.transpose(out, (1, 0, 2, 3, 4)).reshape(b, nb * qb, h * dv)

def _dense_causal_attention(q, k, v, scale, log_decay_cum):
    seq = q.shape[1]
    key_pos = jnp.arange(seq, dtype=jnp.int32)
    cum_k = None if log_decay_cum is None else jnp.transpose(log_decay_cum, (0, 2, 1))

    def block(start):
        qb = lax.dynamic_slice_in_dim(q, start, Q_BLOCK, axis=1)
        s = jnp.einsum('bqhd,bkhd->bhqk', qb, k).astype(jnp.float32) * scale
        if cum_k is not None:
            cum_q = lax.dynamic_slice_in_dim(cum_k, start, Q_BLOCK, axis=2)
            s = s + (cum_q[..., :, None] - cum_k[..., None, :])
        q_pos = start + jnp.arange(Q_BLOCK, dtype=jnp.int32)
        s = jnp.where(key_pos[None, :] <= q_pos[:, None], s, -jnp.inf)
        p = jax.nn.softmax(s, axis=-1).astype(v.dtype)
        return jnp.einsum('bhqk,bkhd->bqhd', p, v)

    return _sweep_blocks(block, seq)

def _dsa_attention(q, k_sh, v_sh, iq, ik, iw, positions, slopes, topk):
    seq = q.shape[1]
    key_pos = jnp.arange(seq, dtype=jnp.int32)
    scale = HEAD_DIM ** -0.5
    gather = jax.vmap(lambda table, idx: table[idx])

    def block(start):
        qb = lax.dynamic_slice_in_dim(q, start, Q_BLOCK, axis=1)
        iqb = lax.dynamic_slice_in_dim(iq, start, Q_BLOCK, axis=1)
        iwb = lax.dynamic_slice_in_dim(iw, start, Q_BLOCK, axis=1).astype(jnp.float32)
        pq = lax.dynamic_slice_in_dim(positions, start, Q_BLOCK, axis=1)
        q_pos = start + jnp.arange(Q_BLOCK, dtype=jnp.int32)
        causal = key_pos[None, :] <= q_pos[:, None]
        idx_logit = jnp.einsum('bqhe,bke->bqhk', iqb, ik).astype(jnp.float32)
        score = jnp.einsum('bqhk,bqh->bqk', jax.nn.relu(idx_logit), iwb)
        score = jnp.where(causal[None], score, -jnp.inf)
        _, sel = lax.top_k(score, topk)
        k_sel = gather(k_sh, sel)
        v_sel = gather(v_sh, sel)
        p_sel = gather(positions, sel)
        s = jnp.einsum('bqhd,bqkd->bhqk', qb, k_sel).astype(jnp.float32) * scale
        dist = jnp.abs(pq[:, :, None] - p_sel).astype(jnp.float32)
        s = s - slopes[None, :, None, None] * dist[:, None]
        valid = sel <= q_pos[None, :, None]
        s = jnp.where(valid[:, None], s, -jnp.inf)
        p = jax.nn.softmax(s, axis=-1).astype(v_sh.dtype)
        return jnp.einsum('bhqk,bqkd->bqhd', p, v_sel)

    return _sweep_blocks(block, seq)

def _mixer(x, positions, w_in, b_gate, b_forget, q_norm, kv_norm, w_uq, w_ukv, w_branch, w_out, slopes, topk):
    bsz, seq, _ = x.shape
    z = x @ w_in
    (c_q, c_kv, k_rope, f_q, f_k, f_v, f_logit, s_q, s_k, s_v, i_q, i_k, i_w, gate_logit) = _split_cols(z)
    q = (_rmsnorm(c_q, q_norm) @ w_uq).reshape(bsz, seq, MLA_HEADS, MLA_NOPE + MLA_ROPE)
    kv = (_rmsnorm(c_kv, kv_norm) @ w_ukv).reshape(bsz, seq, MLA_HEADS, MLA_NOPE + MLA_V)
    q = jnp.concatenate([q[..., :MLA_NOPE], _rope(q[..., MLA_NOPE:], positions)], -1)
    k_r = jnp.broadcast_to(_rope(k_rope[:, :, None, :], positions), (bsz, seq, MLA_HEADS, MLA_ROPE))
    k = jnp.concatenate([kv[..., :MLA_NOPE], k_r], -1)
    o_mla = _dense_causal_attention(q, k, kv[..., MLA_NOPE:], (MLA_NOPE + MLA_ROPE) ** -0.5, None)
    log_f = jax.nn.log_sigmoid((f_logit + b_forget).astype(jnp.float32))
    heads = lambda t, h: t.reshape(bsz, seq, h, HEAD_DIM)
    o_fox = _dense_causal_attention(heads(f_q, FOX_HEADS), heads(f_k, FOX_HEADS), heads(f_v, FOX_HEADS),
                                    HEAD_DIM ** -0.5, jnp.cumsum(log_f, axis=1))
    o_dsa = _dsa_attention(heads(s_q, DSA_HEADS), s_k, s_v, i_q.reshape(bsz, seq, IDX_HEADS, IDX_DIM),
                           i_k, i_w, positions, slopes, topk)
    branches = jnp.stack([o_mla, o_fox, o_dsa], axis=2)
    proj = jnp.einsum('bsnc,ncd->bsnd', branches, w_branch)
    gates = jax.nn.sigmoid(gate_logit.reshape(bsz, seq, N_BRANCH, D_MODEL) + b_gate)
    merged = jnp.einsum('bsnd,bsnd->bsd', gates, proj)
    return merged @ w_out

def _conv_glu_ffn(x, w_up, conv_w, conv_b, w_down):
    seq = x.shape[1]
    u = x @ w_up
    gate, val = u[..., :D_FF], u[..., D_FF:]
    gp = jnp.pad(gate, ((0, 0), (CONV_WIDTH - 1, 0), (0, 0)))
    conv = conv_b
    for j in range(CONV_WIDTH):
        conv = conv + gp[:, j:j + seq] * conv_w[j]
    return (jax.nn.gelu(conv, approximate=False) * val) @ w_down

def setup_inputs(seed: int = 0) -> dict:
    key = jax.random.key(seed)
    ks = jax.random.split(key, 20)
    f32 = jnp.float32
    nrm = lambda k, shape, scale: jax.random.normal(k, shape, f32) * scale
    x = nrm(ks[0], (BATCH, SEQ, D_MODEL), 1.0)
    start = jax.random.randint(ks[1], (BATCH, 1), 0, 1024, dtype=jnp.int32)
    positions = start + jnp.arange(SEQ, dtype=jnp.int32)[None, :]
    w_in = nrm(ks[2], (DEPTH, D_MODEL, D_IN), D_MODEL ** -0.5)
    b_gate = nrm(ks[3], (DEPTH, N_BRANCH, D_MODEL), 0.02)
    b_forget = 1.0 + 3.0 * jax.random.uniform(ks[4], (DEPTH, FOX_HEADS), f32)
    mla_q_norm = 1.0 + nrm(ks[5], (DEPTH, MLA_Q_RANK), 0.02)
    mla_kv_norm = 1.0 + nrm(ks[6], (DEPTH, MLA_KV_RANK), 0.02)
    mla_w_uq = nrm(ks[7], (DEPTH, MLA_Q_RANK, MLA_HEADS * (MLA_NOPE + MLA_ROPE)), MLA_Q_RANK ** -0.5)
    mla_w_ukv = nrm(ks[8], (DEPTH, MLA_KV_RANK, MLA_HEADS * (MLA_NOPE + MLA_V)), MLA_KV_RANK ** -0.5)
    w_branch = nrm(ks[9], (DEPTH, N_BRANCH, BRANCH_WIDTH, D_MODEL), DEEPNORM_BETA * BRANCH_WIDTH ** -0.5)
    w_out = nrm(ks[10], (DEPTH, D_MODEL, D_MODEL), DEEPNORM_BETA * D_MODEL ** -0.5)
    ln1_g = 1.0 + nrm(ks[11], (DEPTH, D_MODEL), 0.02)
    ln1_b = nrm(ks[12], (DEPTH, D_MODEL), 0.02)
    ffn_w_up = nrm(ks[13], (DEPTH, D_MODEL, 2 * D_FF), D_MODEL ** -0.5)
    ffn_conv_w = nrm(ks[14], (DEPTH, CONV_WIDTH, D_FF), CONV_WIDTH ** -0.5)
    ffn_conv_b = nrm(ks[15], (DEPTH, D_FF), 0.02)
    ffn_w_down = nrm(ks[16], (DEPTH, D_FF, D_MODEL), DEEPNORM_BETA * D_FF ** -0.5)
    ln2_g = 1.0 + nrm(ks[17], (DEPTH, D_MODEL), 0.02)
    ln2_b = nrm(ks[18], (DEPTH, D_MODEL), 0.02)
    return {'x': x, 'positions': positions, 'w_in': w_in, 'b_gate': b_gate, 'b_forget': b_forget,
            'mla_q_norm': mla_q_norm, 'mla_kv_norm': mla_kv_norm, 'mla_w_uq': mla_w_uq, 'mla_w_ukv': mla_w_ukv,
            'w_branch': w_branch, 'w_out': w_out, 'ln1_g': ln1_g, 'ln1_b': ln1_b,
            'ffn_w_up': ffn_w_up, 'ffn_conv_w': ffn_conv_w, 'ffn_conv_b': ffn_conv_b, 'ffn_w_down': ffn_w_down,
            'ln2_g': ln2_g, 'ln2_b': ln2_b}

def reference(x, positions, w_in, b_gate, b_forget, mla_q_norm, mla_kv_norm, mla_w_uq, mla_w_ukv,
              w_branch, w_out, ln1_g, ln1_b, ffn_w_up, ffn_conv_w, ffn_conv_b, ffn_w_down, ln2_g, ln2_b):
    seq = x.shape[1]
    topk = min(DSA_MAX_TOPK, seq // 4)
    slopes = _alibi_slopes(DSA_HEADS)
    for l in range(DEPTH):
        y = _mixer(x, positions, w_in[l], b_gate[l], b_forget[l], mla_q_norm[l], mla_kv_norm[l],
                   mla_w_uq[l], mla_w_ukv[l], w_branch[l], w_out[l], slopes, topk)
        x = _layernorm(DEEPNORM_ALPHA * x + y, ln1_g[l], ln1_b[l])
        y = _conv_glu_ffn(x, ffn_w_up[l], ffn_conv_w[l], ffn_conv_b[l], ffn_w_down[l])
        x = _layernorm(DEEPNORM_ALPHA * x + y, ln2_g[l], ln2_b[l])
    return x


_drawn_inputs = setup_inputs


def setup_inputs(seed=0):
    import zlib

    import numpy as np

    out = dict(_drawn_inputs(seed))
    spreads = {}
    factors = {'b_gate': 8.0, 'mla_q_norm': 8.0, 'mla_kv_norm': 8.0, 'ffn_conv_b': 8.0}
    for name, (base, spread) in spreads.items():
        noise = np.random.default_rng([zlib.crc32(name.encode()), seed]).standard_normal(out[name].shape)
        drawn = base * np.exp(spread * noise) if base else spread * noise
        out[name] = __import__('jax').numpy.asarray(drawn.astype(out[name].dtype))
    for name, factor in factors.items():
        out[name] = (out[name] * factor).astype(out[name].dtype)
    return out
```

```python
from contextlib import ExitStack

import numpy as np

import concourse.bass as bass
from concourse import mybir

F32 = mybir.dt.float32
F32R = mybir.dt.float32r
BF16 = mybir.dt.bfloat16
I32 = mybir.dt.int32
ACT = mybir.ActivationFunctionType
ALU = mybir.AluOpType
AX = mybir.AxisListType

P = 128
T = 256
NT = T // P
DM = 1024
KD = DM // P
H = 8
NB = 3
HD = 64
ROPE = 32
HALF = ROPE // 2
QK = HD + ROPE
QR = 192
KVR = 128
IH, IDIM = 8, 32
DFF = 2816
FT = DFF // P
TOPK = T // 4
DEPTH = 2
ALPHA = float((2 * DEPTH) ** 0.25)
LN_EPS, RMS_EPS = 1e-5, 1e-6
THETA = 10000.0

WIDTHS = (QR, KVR, ROPE, H * HD, H * HD, H * HD, H, H * HD, HD, HD, IH * IDIM, IDIM, IH, NB * DM)
OFFS = [sum(WIDTHS[:i]) for i in range(len(WIDTHS) + 1)]
(C_CQ, C_CKV, C_KR, C_FQ, C_FK, C_FV, C_FL, C_SQ, C_SK, C_SV, C_IQ, C_IK, C_IW, C_GATE, DIN) = OFFS
ZW = C_GATE
NZ = 6
ZC = ZW // NZ

PANEL = 2048
Z_AT = [0, 2, 4, 6, 12, 14]
UQ_AT, UKV_AT = 8, 10
GATE_AT = 16
BR_AT = GATE_AT + NB * KD // 2
OUT_AT = BR_AT + 2 * NB
UP_AT = OUT_AT + 4
DOWN_AT = UP_AT + FT
DOWN_K = [4, 4, 4, 4, 4, 2]
NP = DOWN_AT + 2 * len(DOWN_K)
RAW = 3
assert NP % 2 == 0 and NP % RAW == 0

MASKED = -1e30
LOWEST = -3.0e38
TAKEN = -3.3e38
SLOTS = NB * H
LAG_S, LAG_T, LAG_V = 1, 2, 3

ODD = {0: ("iq", 0), 1: ("ik", 0), 2: ("cum", 0)}
ODD.update({3 + n: ("index", n) for n in range(6)})
ODD.update({H * (b + 1) + LAG_V + t: ("turn", NT * b + t) for b in range(NB) for t in range(NT)})
ODD_ORDER = sorted(ODD)
ODD_NO = {s: i for i, s in enumerate(ODD_ORDER)}
N_ODD = len(ODD)
LAST_SLOT = max(ODD_ORDER)

B_GATE, B_S, B_PT, B_QK, B_ODD, B_O = (0, 1), 2, 3, 4, 5, (6, 7)
B_PROJ = (0, 1, 4)
B_R = ((2, 3), (0, 1))
B_X = ((4, 5), (6, 7))
B_LAT = (4, 5)
B_Z = ((0, 1), (2, 3), (0, 1), (2, 3), (4, 5), (6, 7))

PER = dict(
    weights_hi=NP, weights_lo=NP, panel_used=NP,
    x_ready=2 * NT, x_turned=2 * NT, x_hi_ready=2 * NT, x_lo_ready=2 * NT,
    vectors_turned=1, vectors_ready=1, gate_bias_ready=1,
    z_product=NZ, z_even_ready=NZ, z_odd_ready=NZ,
    latent_squares=1, latent_rms=1, latents_normed=1, latents_turned=1, latents_scaled=1, latents_hi=1, latents_lo=1,
    mla_q_product=1, mla_q_ready=NT, rotated=1, mla_kv_product=2, mla_kv_even_ready=2, mla_kv_odd_ready=2,
    forget_logits_ready=1, forget_logs_ready=1, log_forgets_ready=1, index_keys_copied=1, decay_operands_ready=1,
    gate_product=SLOTS // 2, gate_ready=SLOTS, head_turned=SLOTS, head_ready=SLOTS,
    scores_ready=SLOTS, maxima_ready=SLOTS, probs_ready=SLOTS, probs_turned=SLOTS, turned_probs_ready=SLOTS, head_output=SLOTS, outputs_normed=NB,
    odd_product=N_ODD, odd_job_read=N_ODD, outputs_lo_ready=NB * NT, index_head_added=6, index_masked=NT, selection_ready=1,
    proj_product=NB * KD * 3 // 4, proj_gated=NB * KD, merged_ready=KD, merged_hi_ready=KD, merged_lo_ready=KD,
    residual_product=4, variances_ready=2 * NT, deviations_ready=2 * NT, norm_scales_ready=2 * NT, normed_ready=2 * NT,
    conv_first_tap=FT, conv_ready=FT, gelu_ready=FT, hidden_ready=FT, hidden_hi_ready=FT, hidden_lo_ready=FT,
)


def build_program(nc, x, positions, w_in, b_gate, b_forget, q_norm, kv_norm, w_uq, w_ukv, w_branch, w_out,
                  ln1_g, ln1_b, w_up, conv_w, conv_b, w_down, ln2_g, ln2_b, out):
    ctx = ExitStack()
    with ctx:
        def sb(name, shape, dt=F32):
            return ctx.enter_context(nc.sbuf_tensor(name, shape, dt))

        def sem(name):
            return ctx.enter_context(nc.semaphore(name))

        s_weights_hi = sem("weights_hi")
        s_weights_lo = sem("weights_lo")
        s_panel_used = sem("panel_used")
        s_x_ready = sem("x_ready")
        s_x_turned = sem("x_turned")
        s_x_hi_ready = sem("x_hi_ready")
        s_x_lo_ready = sem("x_lo_ready")
        s_vectors_turned = sem("vectors_turned")
        s_vectors_ready = sem("vectors_ready")
        s_gate_bias_ready = sem("gate_bias_ready")
        s_z_product = sem("z_product")
        s_z_even_ready = sem("z_even_ready")
        s_z_odd_ready = sem("z_odd_ready")
        s_latent_squares = sem("latent_squares")
        s_latent_rms = sem("latent_rms")
        s_latents_normed = sem("latents_normed")
        s_latents_turned = sem("latents_turned")
        s_latents_scaled = sem("latents_scaled")
        s_latents_hi = sem("latents_hi")
        s_latents_lo = sem("latents_lo")
        s_mla_q_product = sem("mla_q_product")
        s_mla_q_ready = sem("mla_q_ready")
        s_rotated = sem("rotated")
        s_mla_kv_product = sem("mla_kv_product")
        s_mla_kv_even_ready = sem("mla_kv_even_ready")
        s_mla_kv_odd_ready = sem("mla_kv_odd_ready")
        s_forget_logits_ready = sem("forget_logits_ready")
        s_forget_logs_ready = sem("forget_logs_ready")
        s_log_forgets_ready = sem("log_forgets_ready")
        s_index_keys_copied = sem("index_keys_copied")
        s_decay_operands_ready = sem("decay_operands_ready")
        s_gate_product = sem("gate_product")
        s_gate_ready = sem("gate_ready")
        s_head_turned = sem("head_turned")
        s_head_ready = sem("head_ready")
        s_scores_ready = sem("scores_ready")
        s_maxima_ready = sem("maxima_ready")
        s_probs_ready = sem("probs_ready")
        s_probs_turned = sem("probs_turned")
        s_turned_probs_ready = sem("turned_probs_ready")
        s_head_output = sem("head_output")
        s_outputs_normed = sem("outputs_normed")
        s_odd_product = sem("odd_product")
        s_odd_job_read = sem("odd_job_read")
        s_outputs_lo_ready = sem("outputs_lo_ready")
        s_index_head_added = sem("index_head_added")
        s_index_masked = sem("index_masked")
        s_selection_ready = sem("selection_ready")
        s_proj_product = sem("proj_product")
        s_proj_gated = sem("proj_gated")
        s_merged_ready = sem("merged_ready")
        s_merged_hi_ready = sem("merged_hi_ready")
        s_merged_lo_ready = sem("merged_lo_ready")
        s_residual_product = sem("residual_product")
        s_variances_ready = sem("variances_ready")
        s_deviations_ready = sem("deviations_ready")
        s_norm_scales_ready = sem("norm_scales_ready")
        s_normed_ready = sem("normed_ready")
        s_conv_first_tap = sem("conv_first_tap")
        s_conv_ready = sem("conv_ready")
        s_gelu_ready = sem("gelu_ready")
        s_hidden_ready = sem("hidden_ready")
        s_hidden_hi_ready = sem("hidden_hi_ready")
        s_hidden_lo_ready = sem("hidden_lo_ready")
        loaded = [ctx.enter_context(nc.semaphore(f"w_loaded{i}")) for i in range(RAW)]
        s_in = ctx.enter_context(nc.semaphore("inputs_loaded"))
        s_vecs = ctx.enter_context(nc.semaphore("vectors_loaded"))
        s_gb = ctx.enter_context(nc.semaphore("norm_vectors_loaded"))
        s_const = ctx.enter_context(nc.semaphore("constants_ready"))
        s_setup = ctx.enter_context(nc.semaphore("setup_steps"))
        s_out = ctx.enter_context(nc.semaphore("outputs_stored"))
        BEFORE = dict(weights_lo=RAW)

        def at(name, l, count):
            return l * PER[name] + count + BEFORE.get(name, 0)

        ps = ctx.enter_context(nc.psum_tensor("ps", [P, 8, 512], F32))

        raw = sb("raw", [P, RAW, PANEL])
        w_hi = sb("w_hi", [P, 2, PANEL], F32R)
        w_lo = sb("w_lo", [P, 2, PANEL], F32R)
        x_tok = sb("x_tok", [P, NT, DM])
        xt_hi = sb("xt_hi", [P, KD, T], F32R)
        xt_lo = sb("xt_lo", [P, KD, T], F32R)
        ident = sb("ident", [P, P])
        ident_b = sb("ident_b", [P, P], BF16)
        mask_b = sb("mask_b", [P, P], BF16)
        tri = sb("tri", [P, T])
        dist = sb("dist", [P, NT, T])
        cos = sb("cos_t", [P, NT, HALF])
        sin = sb("sin_t", [P, NT, HALF])
        vecs = sb("vecs", [P, P])
        vec_t = sb("vec_t", [P, P])
        bg2 = sb("bg2", [P, NB * KD])
        bfor = sb("bfor", [P, H])
        eps = sb("eps", [P, 2])
        ot_hi = sb("ot_hi", [P, NB * 4, T], F32R)
        ot_lo = sb("ot_lo", [P, NB * 4, T], F32R)
        group = sb("group", [P, 4])
        waited = sb("waited", [P, 1])
        V_CW, V_CB, V_BG = 0, 3 * FT, 4 * FT
        V_QN = V_BG + NB * KD
        V_KN = V_QN + 2
        V_END = V_KN + 1

        def sized(stack):
            return lambda name, shape, dt=F32: stack.enter_context(nc.sbuf_tensor(name, shape, dt))

        with ExitStack() as over:
            so = sized(over)
            mg_hi = so("mg_hi", [P, KD, T], F32R)
            mg_lo = so("mg_lo", [P, KD, T], F32R)

        with ExitStack() as att:
            sa = sized(att)
            z1 = sa("z1", [P, NT, ZW])
            gates = sa("gates", [P, NB * KD, T])
            with ExitStack() as over:
                so = sized(over)
                merged = so("merged", [P, KD, T])
                gated = so("gated", [P, 2, T])
            q_tok = sa("q_tok", [P, NT, H * QK])
            k_tok = sa("k_tok", [P, NT, H * QK])
            with ExitStack() as over:
                so = sized(over)
                o_tok = so("o_tok", [P, NT, H * HD])
            v_tok = sa("v_tok", [P, NT, H * HD])
            fq_aug = sa("fq_aug", [P, NT, H, HD + 2])
            fk_aug = sa("fk_aug", [P, NT, H, HD + 2])
            rsum = sa("rsum", [P, NB, NT, H])
            rinv = sa("rinv", [P, NT, H])
            small = sa("small", [P, 16])
            fx = sa("fx", [P, NT, H])
            fe = sa("fe", [P, NT, H])
            fl = sa("fl", [P, NT, H])
            with ExitStack() as lat:
                sl = sized(lat)
                c_f = sl("c_f", [P, 3, T])
                c_hi = sl("c_hi", [P, 3, T], F32R)
                c_lo = sl("c_lo", [P, 3, T], F32R)
                cn = sl("cn", [P, NT, QR + KVR])
                rot = sl("rot", [P, 4, NT, H, HALF])
                krot = sl("krot", [P, 4, NT, HALF])
                kr = sl("kr", [P, NT, ROPE])
            with ExitStack() as heads:
                sh = sized(heads)
                qks = sh("qks", [P, 2, 2, T])
                prob = sh("prob", [P, 2, 3 * P])
                pts = sh("pts", [P, 2, 3 * P])
                ikd = sh("ikd", [P, NT, P])
                iqt = sh("iqt", [P, 2, T])
                ikt = sh("ikt", [P, 4, T])
                skt = sh("skt", [HD, T])
                rel = sh("rel", [P, 2, 512])
                with ExitStack() as over:
                    ssc = sized(over)("ssc", [P, 3 * P])
                ix = sh("ix", [P, 3 * P])
                ixw = sh("ixw", [P, 3 * P])
                top8 = sh("top8", [P, 8])
                selm = sh("selm", [P, 3 * P], BF16)
                negm = sh("negm", [P, 2, NT])

        with ExitStack() as ffn:
            sf = sized(ffn)
            ht_hi = sf("ht_hi", [P, FT, T], F32R)
            ht_lo = sf("ht_lo", [P, FT, T], F32R)
            cv = sf("cv", [P, 2, T])
            ge = sf("ge", [P, 2, T])
            hf = sf("hf", [P, 2, T])
            res = sf("res", [P, NT, DM])
            ln_g = sf("ln_g", [P, DM])
            ln_b = sf("ln_b", [P, DM])
            stats = sf("stats", [P, NT, 2, 6])
            mv = sf("mv", [P, NT, 2])
            lnv = sf("lnv", [P, NT, 4])

        with ExitStack() as start:
            ss_ = sized(start)
            pos_row = ss_("pos_row", [P, T], I32)
            pos_col = ss_("pos_col", [P, NT], I32)
            pos_f = ss_("pos_f", [P, T])
            pos_c = ss_("pos_c", [P, NT])
            freq = ss_("freq", [P, HALF])
            ang = ss_("ang", [P, NT, HALF])
            turns = ss_("turns", [P, NT, HALF])
            angc = ss_("angc", [P, NT, HALF])


        SPAN = (slice(0, P), slice(P, 3 * P))
        HEAD_ROWS = (QK, HD + 2, HD)
        ROUND = 1.5 * 2 ** 23
        TWO_PI = (6.28125, 0.0019340515136718750, float(np.float32(2 * np.pi - 6.28125 - 0.0019340515136718750)))
        PI_BELOW = 3.1415925
        N_CONST = 7
        N_VECS = 7
        s_trig = ctx.enter_context(nc.semaphore("rotations_ready"))
        s_pool = ctx.enter_context(nc.semaphore("gpsimd_constants"))

        def f_par(slot):
            return slot

        def column(w, c0, f):
            return w[:, c0 + f:c0 + f + 1] if isinstance(f, int) else w[:, bass.ds(f + c0, 1)]

        def tile_at(w, f):
            return w[:, f, :] if isinstance(f, int) else w[:, bass.ds(f, 1), :].rearrange("p a t -> p (a t)")

        def x_psum(t):
            return ps[:, B_X[t][0]:B_X[t][0] + 2, :].rearrange("p b (k t) -> p (b k) t", t=P)

        def keys_values(c, t):
            src = ps[:, 2 * c + t, :].rearrange("p (h n) -> p h n", n=2 * HD)
            k = k_tok[:, t, 4 * QK * c:4 * QK * (c + 1)].rearrange("p (h n) -> p h n", n=QK)
            v = v_tok[:, t, 4 * HD * c:4 * HD * (c + 1)].rearrange("p (h n) -> p h n", n=HD)
            return k[:, :, 0:HD], src[:, :, 0:HD], v, src[:, :, HD:2 * HD]

        def proj_psum(u):
            return ps[:, B_PROJ[u % len(B_PROJ)], 0:T]

        inv_freq = (np.float32(THETA) ** (-np.arange(HALF, dtype=np.float32) / np.float32(HALF))).astype(np.float32)

        def loaded_count(l, p):
            return 32 * (l * (NP // RAW) + p // RAW + 1)

        def weight_rows(w, l, r0, nr, c0, ncol):
            return w[bass.ds(l, 1), r0:r0 + nr, c0:c0 + ncol].rearrange("a (k p) n -> p (a k) n", p=P)

        def view(buf, slot, k, ncol, k0=0, nk=None):
            nk = k - k0 if nk is None else nk
            return buf[:, slot, 0:k * ncol].rearrange("p (k n) -> p k n", k=k)[:, k0:k0 + nk, :]

        def halves(l, p):
            s = p % RAW

            def cut(w, r0, k, c0, ncol):
                a = k // 2
                return [(view(raw, s, k, ncol, 0, a), weight_rows(w, l, r0, a * P, c0, ncol)),
                        (view(raw, s, k, ncol, a), weight_rows(w, l, r0 + a * P, (k - a) * P, c0, ncol))]

            for i, at in enumerate(Z_AT):
                if p in (at, at + 1):
                    return cut(w_in, 512 * (p - at), 4, ZC * i, ZC)
            if p in (UQ_AT, UQ_AT + 1):
                nr = P if p == UQ_AT else QR - P
                r0 = P * (p - UQ_AT)
                return [(raw[0:nr, s, c:c + 384],
                         w_uq[bass.ds(l, 1), r0:r0 + nr, c:c + 384].rearrange("a p n -> p (a n)")) for c in (0, 384)]
            if p in (UKV_AT, UKV_AT + 1):
                c0 = 512 * (p - UKV_AT)
                return [(raw[:, s, c:c + 256],
                         w_ukv[bass.ds(l, 1), :, c0 + c:c0 + c + 256].rearrange("a p n -> p (a n)")) for c in (0, 256)]
            if p < BR_AT:
                return cut(w_in, 0, KD, C_GATE + T * (p - GATE_AT), 256)
            if p < OUT_AT:
                n, c = divmod(p - BR_AT, 2)
                wb = w_branch[bass.ds(l, 1), n].rearrange("a k n -> a k n")
                return [(view(raw, s, 4, 512, 2 * i, 2),
                         wb[:, 256 * i:256 * i + 256, 512 * c:512 * c + 512].rearrange("a (k p) n -> p (a k) n", p=P))
                        for i in range(2)]
            if p < UP_AT:
                c, kh = divmod(p - OUT_AT, 2)
                return cut(w_out, 512 * kh, 4, 512 * c, 512)
            if p < DOWN_AT:
                return up_halves(l, s, p - UP_AT)
            c, g = divmod(p - DOWN_AT, len(DOWN_K))
            return cut(w_down, P * sum(DOWN_K[:g]), DOWN_K[g], 512 * c, 512)

        def up_halves(l, s, f):
            return [(view(raw, s, KD, 2 * P)[:, :, P * i:P * i + P],
                     w_up[bass.ds(l, 1), :, bass.ds(f * P + DFF * i, P)].rearrange("a (k p) n -> p (a k) n", p=P))
                    for i in range(2)]

        def panel_extent(p):
            for at in Z_AT:
                if p in (at, at + 1):
                    return P, 4 * ZC
            if p in (UQ_AT, UQ_AT + 1):
                return (P if p == UQ_AT else QR - P), H * QK
            if p in (UKV_AT, UKV_AT + 1):
                return P, 512
            if p >= DOWN_AT:
                return P, 512 * DOWN_K[(p - DOWN_AT) % len(DOWN_K)]
            return P, PANEL

        block = ctx.enter_context(nc.Block())

        @block.sync
        def _(sp):
            sp.dma_start(x_tok[:], x[0].rearrange("(t p) d -> p t d", p=P)).then_inc(s_in, 16)
            sp.dma_start(pos_row[:], positions.partition_broadcast(P)).then_inc(s_in, 16)
            sp.dma_start(pos_col[:], positions.rearrange("a (t p) -> p (a t)", p=P),
                         allow_slow_non_contiguous=True).then_inc(s_in, 16)
            with sp.Fori(0, DEPTH) as l:
                one = bass.ds(l, 1)
                fill = [
                    (vecs[V_CW:V_CB, :], conv_w[one].rearrange("a j (f n) -> (a j f) n", n=P)),
                    (vecs[V_CB:V_BG, :], conv_b[one].rearrange("a (f n) -> (a f) n", n=P)),
                    (vecs[V_BG:V_QN, :], b_gate[one].rearrange("a j (f n) -> (a j f) n", n=P)),
                    (vecs[V_QN:V_QN + 1, :], q_norm[one, 0:P]),
                    (vecs[V_QN + 1:V_QN + 2, 0:QR - P], q_norm[one, P:QR]),
                    (vecs[V_KN:V_END, :], kv_norm[one]),
                    (bfor[:], b_forget[one].rearrange("a h -> (a h)").partition_broadcast(P)),
                ]
                sp.wait_ge(s_setup, 1)
                for dst, src in fill:
                    sp.dma_start(dst, src).then_inc(s_vecs, 16)
                for p in range(NP):
                    sp.wait_ge(s_weights_lo, at("weights_lo", l, p - RAW + 1))
                    for i, (dst, src) in enumerate(halves(l, p)):
                        if (p, i) == (OUT_AT, 1):
                            sp.wait_ge(s_vectors_ready, at("vectors_ready", l, 1))
                        if (p, i) == (OUT_AT + 1, 1):
                            sp.wait_ge(s_log_forgets_ready, at("log_forgets_ready", l, 1))
                        sp.dma_start(dst, src).then_inc(loaded[p % RAW], 16)
                    if p in (OUT_AT + 1, DOWN_AT + 1):
                        g, b = (ln1_g, ln1_b) if p < UP_AT else (ln2_g, ln2_b)
                        second = p > UP_AT
                        if second:
                            sp.wait_ge(s_x_ready, at("x_ready", l, 2 * NT))
                        else:
                            sp.wait_ge(s_merged_lo_ready, at("merged_lo_ready", l, KD))
                        sp.dma_start(ln_g[:], g[one].rearrange("a d -> (a d)").partition_broadcast(P)).then_inc(s_gb, 16)
                        sp.dma_start(ln_b[:], b[one].rearrange("a d -> (a d)").partition_broadcast(P)).then_inc(s_gb, 16)
            for t in range(NT):
                sp.wait_ge(s_x_ready, DEPTH * PER["x_ready"] + t + 1)
                sp.dma_start(out[0, P * t:P * t + P, :], x_tok[:, t, :]).then_inc(s_out, 16)
            sp.wait_ge(s_out, 16 * NT)

        @block.tensor
        def _(pe):
            def product(dst, a_hi, a_lo, b_hi, b_lo, first, last):
                pe.matmul(dst, a_hi, b_hi, start=first, stop=False)
                pe.matmul(dst, a_hi, b_lo, start=False, stop=False)
                return pe.matmul(dst, a_lo, b_hi, start=False, stop=last)

            def panel(l, p, k, ncol):
                pe.wait_ge(s_weights_lo, at("weights_lo", l, p + 1))
                return view(w_hi, p % 2, k, ncol), view(w_lo, p % 2, k, ncol)

            def by_token(l, p, k_of, nk, ncol, lhs, banks, first, last):
                whi, wlo = panel(l, p, nk, ncol)
                for t in range(NT):
                    tok = slice(P * t, P * t + P)
                    for k in range(nk):
                        kk = k_of + k
                        ins = product(ps[:, banks[t], 0:ncol], lhs[0][:, kk, tok], lhs[1][:, kk, tok],
                                      whi[:, k, :], wlo[:, k, :], first and k == 0, last and k == nk - 1)
                    yield t, ins

            def turn_x(l, j):
                for t in range(NT):
                    pe.wait_ge(s_x_ready, at("x_ready", l, NT * j + t + 1))
                    for k in range(KD):
                        ins = pe.transpose(ps[:, B_X[t][k // 4], P * (k % 4):P * (k % 4) + P],
                                           x_tok[:, t, P * k:P * k + P], ident[:])
                    ins.then_inc(s_x_turned, 1)

            def z_chunk(l, i):
                if i in (2, 3):
                    pe.wait_ge(s_z_even_ready, at("z_even_ready", l, i - 1))
                    pe.wait_ge(s_z_odd_ready, at("z_odd_ready", l, i - 1))
                if i in (4, 5):
                    pe.wait_ge(s_mla_q_ready, at("mla_q_ready", l, i - 3))
                for half in range(2):
                    p = Z_AT[i] + half
                    for t, ins in by_token(l, p, 4 * half, 4, ZC, (xt_hi, xt_lo), B_Z[i], half == 0, half == 1):
                        if half == 1 and t == 0:
                            ins.then_inc(s_z_product, 1)
                    ins.then_inc(s_panel_used, 1)

            def latents(l):
                pe.wait_ge(s_latents_normed, at("latents_normed", l, 1))
                for t in range(NT):
                    pe.transpose(ps[:, B_LAT[0], P * t:P * t + P], cn[:, t, 0:P], ident[:])
                    pe.transpose(ps[:, B_LAT[0], T + P * t:T + P * t + P], cn[:, t, QR:QR + KVR], ident[:])
                    ins = pe.transpose(ps[0:QR - P, B_LAT[1], P * t:P * t + P], cn[:, t, P:QR], ident[:])
                ins.then_inc(s_latents_turned, 1)

            def mla_queries(l):
                pe.wait_ge(s_latents_lo, at("latents_lo", l, 1))
                for half, (n, kk) in enumerate(((P, 0), (QR - P, 2))):
                    p = UQ_AT + half
                    pe.wait_ge(s_weights_lo, at("weights_lo", l, p + 1))
                    for t in range(NT):
                        tok = slice(P * t, P * t + P)
                        for c in range(2):
                            cols = slice(384 * c, 384 * c + 384)
                            ins = product(ps[:, 4 + 2 * t + c, 0:384], c_hi[0:n, kk, tok], c_lo[0:n, kk, tok],
                                          w_hi[0:n, p % 2, cols], w_lo[0:n, p % 2, cols], half == 0, half == 1)
                        if half == 1 and t == 0:
                            ins.then_inc(s_mla_q_product, 1)
                    ins.then_inc(s_panel_used, 1)

            def mla_keys(l):
                for c in range(2):
                    p = UKV_AT + c
                    pe.wait_ge(s_z_even_ready, at("z_even_ready", l, 3 + c))
                    pe.wait_ge(s_z_odd_ready, at("z_odd_ready", l, 3 + c))
                    pe.wait_ge(s_weights_lo, at("weights_lo", l, p + 1))
                    for t in range(NT):
                        tok = slice(P * t, P * t + P)
                        ins = product(ps[:, 2 * c + t, :], c_hi[:, 1, tok], c_lo[:, 1, tok],
                                      w_hi[:, p % 2, 0:512], w_lo[:, p % 2, 0:512], True, True)
                        if t == 0:
                            ins.then_inc(s_mla_kv_product, 1)
                    ins.then_inc(s_panel_used, 1)

            def gate_tile(l, s):
                p = GATE_AT + s // 2
                if s % 2 == 0:
                    pe.wait_ge(s_weights_lo, at("weights_lo", l, p + 1))
                if s == 0:
                    pe.wait_ge(s_mla_kv_even_ready, at("mla_kv_even_ready", l, 1))
                    pe.wait_ge(s_mla_kv_odd_ready, at("mla_kv_odd_ready", l, 1))
                if s >= 2:
                    pe.wait_ge(s_gate_ready, at("gate_ready", l, s - 1))
                whi, wlo = view(w_hi, p % 2, KD, T), view(w_lo, p % 2, KD, T)
                cols = slice(P * (s % 2), P * (s % 2) + P)
                for k in range(KD):
                    ins = product(ps[:, B_GATE[s % 2], 0:T], whi[:, k, cols], wlo[:, k, cols],
                                  xt_hi[:, k, :], xt_lo[:, k, :], k == 0, k == KD - 1)
                if s % 2:
                    ins.then_inc(s_panel_used, 1)
                else:
                    ins.then_inc(s_gate_product, 1)

            def head_operands_ready(l, s):
                if s == 0:
                    pe.wait_ge(s_z_even_ready, at("z_even_ready", l, 5))
                    pe.wait_ge(s_rotated, at("rotated", l, 1))
                    pe.wait_ge(s_mla_kv_even_ready, at("mla_kv_even_ready", l, 2))
                    pe.wait_ge(s_mla_kv_odd_ready, at("mla_kv_odd_ready", l, 2))
                else:
                    pe.wait_ge(s_head_ready, at("head_ready", l, s))
                if s == H:
                    pe.wait_ge(s_decay_operands_ready, at("decay_operands_ready", l, 1))
                    pe.wait_ge(s_odd_job_read, at("odd_job_read", l, ODD_NO[2] + 1))
                if s == 2 * H:
                    pe.wait_ge(s_z_even_ready, at("z_even_ready", l, NZ))
                    pe.wait_ge(s_z_odd_ready, at("z_odd_ready", l, NZ))

            def head_operands(l, s):
                b, h = divmod(s, H)
                for t in range(NT):
                    if b == 0:
                        q, k = (w[:, t, QK * h:QK * h + QK] for w in (q_tok, k_tok))
                    elif b == 1:
                        q, k = fq_aug[:, t, h, :], fk_aug[:, t, h, :]
                    else:
                        q, k = z1[:, t, C_SQ + HD * h:C_SQ + HD * h + HD], None
                    d = HEAD_ROWS[b]
                    ins = pe.transpose(ps[0:d, B_QK, P * t:P * t + P], q, ident[:])
                    if k is not None:
                        ins = pe.transpose(ps[0:d, B_QK, T + P * t:T + P * t + P], k, ident[:])
                ins.then_inc(s_head_turned, 1)

            def odd_job(l, s):
                what, n = ODD[s]
                i = ODD_NO[s]
                if i == 0:
                    pe.wait_ge(s_z_odd_ready, at("z_odd_ready", l, 5))
                    pe.wait_ge(s_z_even_ready, at("z_even_ready", l, NZ))
                    pe.wait_ge(s_z_odd_ready, at("z_odd_ready", l, NZ))
                else:
                    pe.wait_ge(s_odd_job_read, at("odd_job_read", l, i))
                if what == "turn" and n > 0:
                    pe.wait_ge(s_outputs_lo_ready, at("outputs_lo_ready", l, n))
                if what == "iq":
                    for blk in range(2):
                        for t in range(NT):
                            ins = pe.transpose(ps[:, B_ODD, T * blk + P * t:T * blk + P * t + P],
                                               z1[:, t, C_IQ + P * blk:C_IQ + P * blk + P], ident[:])
                elif what == "ik":
                    pe.wait_ge(s_index_keys_copied, at("index_keys_copied", l, 1))
                    for t in range(NT):
                        pe.transpose(ps[:, B_ODD, P * t:P * t + P], ikd[:, t, :], ident[:])
                        ins = pe.transpose(ps[0:HD, B_ODD, T + P * t:T + P * t + P], z1[:, t, C_SK:C_SK + HD], ident[:])
                elif what == "cum":
                    pe.wait_ge(s_log_forgets_ready, at("log_forgets_ready", l, 1))
                    pe.matmul(ps[:, B_ODD, 0:H], tri[:, 0:P], fx[:, 0, :], start=True, stop=True)
                    pe.matmul(ps[:, B_ODD, H:2 * H], tri[:, P:T], fx[:, 0, :], start=True, stop=False)
                    ins = pe.matmul(ps[:, B_ODD, H:2 * H], tri[:, 0:P], fx[:, 1, :], start=False, stop=True)
                elif what == "index":
                    t = 0 if n < 2 else 1
                    hs = range(4 * n, 4 * n + 4) if t == 0 else range(2 * (n - 2), 2 * (n - 2) + 2)
                    keys = P * (t + 1)
                    for j, h in enumerate(hs):
                        ins = pe.matmul(ps[:, B_ODD, keys * j:keys * j + keys], iqt[:, h // 4, P * t:P * t + P],
                                        ikt[:, h % 4, 0:keys], start=True, stop=True)
                else:
                    b, t = divmod(n, NT)
                    pe.wait_ge(s_outputs_normed, at("outputs_normed", l, b + 1))
                    for k in range(4):
                        ins = pe.transpose(ps[:, B_ODD, P * k:P * k + P], o_tok[:, t, P * k:P * k + P], ident[:])
                ins.then_inc(s_odd_product, 1)

            def scores(l, hh):
                b, h = divmod(hh, H)
                bank, buf, d = B_S, hh % 2, HEAD_ROWS[b]
                pe.wait_ge(s_head_ready, at("head_ready", l, hh + 1))
                if hh > 0:
                    pe.wait_ge(s_probs_ready, at("probs_ready", l, hh))
                if hh == 2 * H:
                    pe.wait_ge(s_selection_ready, at("selection_ready", l, 1))
                q = qks[0:d, buf, 0, :]
                k = skt[:, :] if b == 2 else qks[0:d, buf, 1, :]
                pe.matmul(ps[:, bank, 0:P], q[:, 0:P], k[:, 0:P], start=True, stop=False)
                pe.matmul(ps[:, bank, 0:P], ident_b[:], selm[:, 0:P] if b == 2 else mask_b[:], start=False, stop=True)
                pe.matmul(ps[:, bank, P:3 * P], q[:, P:T], k[:, 0:T], start=True, stop=False)
                if b == 2:
                    ins = pe.matmul(ps[:, bank, P:3 * P], ident_b[:], selm[:, P:3 * P], start=False, stop=True)
                else:
                    ins = pe.matmul(ps[:, bank, T:3 * P], ident_b[:], mask_b[:], start=False, stop=True)
                ins.then_inc(s_scores_ready, 1)

            def turn_probs(l, hh):
                pe.wait_ge(s_probs_ready, at("probs_ready", l, hh + 1))
                if hh > 0:
                    pe.wait_ge(s_turned_probs_ready, at("turned_probs_ready", l, hh))
                for i in range(3):
                    ins = pe.transpose(ps[:, B_PT, P * i:P * i + P], prob[:, hh % 2, P * i:P * i + P], ident[:])
                ins.then_inc(s_probs_turned, 1)

            def values(l, hh):
                b, h = divmod(hh, H)
                pe.wait_ge(s_turned_probs_ready, at("turned_probs_ready", l, hh + 1))
                if hh == 0:
                    pe.wait_ge(s_z_even_ready, at("z_even_ready", l, NZ))
                    pe.wait_ge(s_z_odd_ready, at("z_odd_ready", l, NZ))
                elif h == 0:
                    pe.wait_ge(s_outputs_normed, at("outputs_normed", l, b))
                v = [v_tok[:, t, HD * h:HD * h + HD] if b == 0 else
                     z1[:, t, C_FV + HD * h:C_FV + HD * h + HD] if b == 1 else z1[:, t, C_SV:C_SV + HD]
                     for t in range(NT)]
                cols, buf = slice(HD * h, HD * h + HD), hh % 2
                pe.matmul(ps[:, B_O[0], cols], pts[:, buf, 0:P], v[0], start=True, stop=True)
                pe.matmul(ps[:, B_O[1], cols], pts[:, buf, P:T], v[0], start=True, stop=False)
                pe.matmul(ps[:, B_O[1], cols], pts[:, buf, T:3 * P], v[1], start=False, stop=True).then_inc(s_head_output, 1)

            def branch_panel(l, q):
                n, c = divmod(q, 2)
                whi, wlo = panel(l, BR_AT + q, 4, 512)
                if c == 0:
                    pe.wait_ge(s_outputs_lo_ready, at("outputs_lo_ready", l, NT * (n + 1)))
                for jj in range(4):
                    u = 8 * n + 4 * c + jj
                    if u == 0:
                        pe.wait_ge(s_gate_ready, at("gate_ready", l, SLOTS))
                    if u == 2:
                        pe.wait_ge(s_head_ready, at("head_ready", l, SLOTS))
                    if u >= len(B_PROJ):
                        pe.wait_ge(s_proj_gated, at("proj_gated", l, u - len(B_PROJ) + 1))
                    dst = proj_psum(u)
                    for k in range(4):
                        cols = slice(P * jj, P * jj + P)
                        ins = product(dst, whi[:, k, cols], wlo[:, k, cols], ot_hi[:, 4 * n + k, :],
                                      ot_lo[:, 4 * n + k, :], k == 0, k == 3)
                    if jj < 3:
                        ins.then_inc(s_proj_product, 1)
                ins.then_inc(s_panel_used, 1)

            def ffn_up(l, f, slot, first):
                pe.wait_ge(s_weights_lo, at("weights_lo", l, UP_AT + f + 1))
                if not first:
                    pe.wait_ge(s_hidden_ready, at("hidden_ready", l, f - 1))
                bank = f_par(slot)
                whi, wlo = view(w_hi, slot, KD, 2 * P), view(w_lo, slot, KD, 2 * P)
                for i in range(2):
                    for k in range(KD):
                        cols = slice(P * i, P * i + P)
                        ins = product(ps[:, bank, T * i:T * i + T], whi[:, k, cols], wlo[:, k, cols],
                                      xt_hi[:, k, :], xt_lo[:, k, :], k == 0, k == KD - 1)
                ins.then_inc(s_panel_used, 1)

            pe.wait_ge(s_const, N_CONST)
            with pe.Fori(0, DEPTH) as l:
                turn_x(l, 0)
                pe.wait_ge(s_vecs, 16 * N_VECS * (l + 1))
                pe.transpose(ps[:, 2, 0:P], vecs[:], ident[:]).then_inc(s_vectors_turned, 1)
                pe.wait_ge(s_x_lo_ready, at("x_lo_ready", l, NT))
                z_chunk(l, 0)
                pe.wait_ge(s_vectors_ready, at("vectors_ready", l, 1))
                z_chunk(l, 1)
                latents(l)
                z_chunk(l, 2)
                z_chunk(l, 3)
                mla_queries(l)
                mla_keys(l)
                z_chunk(l, 4)
                z_chunk(l, 5)
                for s in range(LAST_SLOT + 1):
                    if s < SLOTS:
                        if s >= 2 * H:
                            head_operands_ready(l, s)
                        gate_tile(l, s)
                        if s < 2 * H:
                            head_operands_ready(l, s)
                        head_operands(l, s)
                    if s in ODD:
                        odd_job(l, s)
                    if 0 <= s - LAG_S < SLOTS:
                        scores(l, s - LAG_S)
                    if 0 <= s - LAG_T < SLOTS:
                        turn_probs(l, s - LAG_T)
                    if 0 <= s - LAG_V < SLOTS:
                        values(l, s - LAG_V)
                    if 0 <= s - SLOTS < 4:
                        branch_panel(l, s - SLOTS)
                branch_panel(l, 4)
                branch_panel(l, 5)
                for c in range(2):
                    for kh in range(2):
                        pe.wait_ge(s_merged_lo_ready, at("merged_lo_ready", l, 4 * kh + 4))
                        for t, ins in by_token(l, OUT_AT + 2 * c + kh, 4 * kh, 4, 512, (mg_hi, mg_lo), B_R[c],
                                               kh == 0, kh == 1):
                            if kh == 1 and t == 0:
                                ins.then_inc(s_residual_product, 1)
                        ins.then_inc(s_panel_used, 1)
                turn_x(l, 1)
                pe.wait_ge(s_x_lo_ready, at("x_lo_ready", l, 2 * NT))
                for f in range(FT):
                    ffn_up(l, f, (UP_AT + f) % 2, f < 2)
                for c in range(2):
                    for g, nk in enumerate(DOWN_K):
                        k0 = sum(DOWN_K[:g])
                        pe.wait_ge(s_hidden_lo_ready, at("hidden_lo_ready", l, FT if c else k0 + nk))
                        for t, ins in by_token(l, DOWN_AT + 6 * c + g, k0, nk, 512, (ht_hi, ht_lo), B_R[c],
                                               g == 0, g == len(DOWN_K) - 1):
                            if g == len(DOWN_K) - 1 and t == 0:
                                ins.then_inc(s_residual_product, 1)
                        ins.then_inc(s_panel_used, 1)

        @block.scalar
        def _(act):
            def split_hi(l, p):
                act.wait_ge(loaded[p % RAW], loaded_count(l, p))
                if p >= 2:
                    act.wait_ge(s_panel_used, at("panel_used", l, p - 1))
                n, ncol = panel_extent(p)
                act.activation(w_hi[0:n, p % 2, 0:ncol], raw[0:n, p % RAW, 0:ncol], ACT.Copy).then_inc(s_weights_hi, 1)

            def x_hi(l, j):
                for t in range(NT):
                    act.wait_ge(s_x_turned, at("x_turned", l, NT * j + t + 1))
                    act.activation(xt_hi[:, :, P * t:P * t + P], x_psum(t), ACT.Copy).then_inc(s_x_hi_ready, 1)

            def z_out(l, i):
                act.wait_ge(s_z_product, at("z_product", l, i + 1))
                act.activation(z1[:, 0, ZC * i:ZC * i + ZC], ps[:, B_Z[i][0], 0:ZC], ACT.Copy).then_inc(s_z_even_ready, 1)

            def gate(l, s):
                if s % 2 == 1:
                    act.wait_ge(s_panel_used, at("panel_used", l, GATE_AT + s // 2 + 1))
                else:
                    act.wait_ge(s_gate_product, at("gate_product", l, s // 2 + 1))
                act.activation(gates[:, s, :], ps[:, B_GATE[s % 2], 0:T], ACT.Tanh,
                                   scale=0.5, bias=bg2[:, s:s + 1]).then_inc(s_gate_ready, 1)

            def head_out(l, s):
                b = s // H
                d = HEAD_ROWS[b]
                act.wait_ge(s_head_turned, at("head_turned", l, s + 1))
                if s >= 2:
                    act.wait_ge(s_scores_ready, at("scores_ready", l, s - 1))
                if b < 2:
                    ins = act.activation(qks[0:d, s % 2, :, :], ps[0:d, B_QK, :].rearrange("p (a t) -> p a t", a=2),
                                         ACT.Copy)
                else:
                    ins = act.activation(qks[0:d, s % 2, 0, :], ps[0:d, B_QK, 0:T], ACT.Copy, scale=HD ** -0.5)
                ins.then_inc(s_head_ready, 1)

            def odd_out(l, s):
                what, n = ODD[s]
                act.wait_ge(s_odd_product, at("odd_product", l, ODD_NO[s] + 1))
                if what == "iq":
                    ins = act.activation(iqt[:], ps[:, B_ODD, :].rearrange("p (b t) -> p b t", b=2), ACT.Copy)
                elif what == "ik":
                    for j in range(4):
                        act.activation(ikt[:, j, :], ps[:, B_ODD, 0:T], ACT.Copy, scale=group[:, j:j + 1])
                    ins = act.activation(skt[:], ps[0:HD, B_ODD, T:2 * T], ACT.Copy)
                elif what == "cum":
                    cum = ps[:, B_ODD, 0:2 * H].rearrange("p (t h) -> p t h", t=NT)
                    act.wait_ge(s_decay_operands_ready, at("decay_operands_ready", l, 1))
                    act.activation(fq_aug[:, :, :, HD], cum, ACT.Copy)
                    ins = act.activation(fk_aug[:, :, :, HD + 1], cum, ACT.Copy, scale=-1.0)
                elif what == "index":
                    if n >= 2:
                        act.wait_ge(s_index_head_added, at("index_head_added", l, n - 1))
                    ins = act.activation(rel[:, n % 2, :], ps[:, B_ODD, :], ACT.Relu)
                else:
                    b, t = divmod(n, NT)
                    ins = act.activation(ot_hi[:, 4 * b:4 * b + 4, P * t:P * t + P],
                                         ps[:, B_ODD, :].rearrange("p (k t) -> p k t", k=4), ACT.Copy)
                ins.then_inc(s_odd_job_read, 1)

            def softmax_exp(l, hh):
                b, h = divmod(hh, H)
                act.wait_ge(s_maxima_ready, at("maxima_ready", l, hh + 1))
                if hh >= 2:
                    act.wait_ge(s_probs_turned, at("probs_turned", l, hh - 1))
                for t in range(NT):
                    cols = SPAN[t]
                    src = ssc[:, cols] if b == 2 else ps[:, B_S, cols]
                    ins = act.activation(prob[:, hh % 2, cols], src, ACT.Exp, bias=negm[:, hh % 2, t:t + 1],
                                         accum_out=rsum[:, b, t, h:h + 1])
                ins.then_inc(s_probs_ready, 1)

            def merged_hi(l, j):
                act.wait_ge(s_merged_ready, at("merged_ready", l, j + 1))
                act.activation(mg_hi[:, j, :], merged[:, j, :], ACT.Copy, scale=0.5).then_inc(s_merged_hi_ready, 1)

            def norm(l, j):
                for t in range(NT):
                    act.wait_ge(s_variances_ready, at("variances_ready", l, NT * j + t + 1))
                    act.activation(lnv[:, t, 0:1], mv[:, t, 1:2], ACT.Sqrt, bias=eps[:, 0:1]).then_inc(s_deviations_ready, 1)
                for t in range(NT):
                    act.wait_ge(s_norm_scales_ready, at("norm_scales_ready", l, NT * j + t + 1))
                    act.activation(res[:, t, :], res[:, t, :], ACT.Identity, scale=lnv[:, t, 1:2],
                                       bias=lnv[:, t, 3:4]).then_inc(s_normed_ready, 1)

            def conv_first(l, f, buf):
                act.wait_ge(s_panel_used, at("panel_used", l, UP_AT + f + 1))
                act.activation(cv[:, buf, :], ps[:, buf, 0:T], ACT.Copy,
                                   scale=column(vec_t, V_CW + 2 * FT, f)).then_inc(s_conv_first_tap, 1)

            def gelu(l, f, buf, first):
                act.wait_ge(s_conv_ready, at("conv_ready", l, f + 1))
                if not first:
                    act.wait_ge(s_hidden_ready, at("hidden_ready", l, f - 1))
                act.activation(ge[:, buf, :], cv[:, buf, :], ACT.Gelu, bias=column(vec_t, V_CB, f)).then_inc(s_gelu_ready, 1)

            def hidden_hi(l, f, buf):
                act.wait_ge(s_hidden_ready, at("hidden_ready", l, f + 1))
                act.activation(tile_at(ht_hi, f), hf[:, buf, :], ACT.Copy).then_inc(s_hidden_hi_ready, 1)

            act.wait_ge(s_setup, 2)
            act.activation(sin[:], ang[:], ACT.Sin)
            act.activation(cos[:], angc[:], ACT.Sin).then_inc(s_trig, 1)
            act.wait_ge(s_const, N_CONST)
            with act.Fori(0, DEPTH) as l:
                split_hi(l, 0)
                x_hi(l, 0)
                act.wait_ge(s_vectors_turned, at("vectors_turned", l, 1))
                act.activation(vec_t[:], ps[:, 2, 0:P], ACT.Copy).then_inc(s_vectors_ready, 1)
                act.wait_ge(s_gate_bias_ready, at("gate_bias_ready", l, 1))
                for p in range(GATE_AT):
                    split_hi(l, p + 1)
                    if p - 1 in Z_AT:
                        z_out(l, Z_AT.index(p - 1))
                    if p == 2:
                        act.wait_ge(s_latent_squares, at("latent_squares", l, 1))
                        act.activation(small[:, 4:6], small[:, 0:2], ACT.Sqrt, scale=1.0 / QR, bias=eps[:, 1:2])
                        act.activation(small[:, 6:8], small[:, 2:4], ACT.Sqrt, scale=1.0 / KVR,
                                           bias=eps[:, 1:2]).then_inc(s_latent_rms, 1)
                    if p == 4:
                        act.wait_ge(s_latents_scaled, at("latents_scaled", l, 1))
                        act.activation(c_hi[:, 0:2, :], c_f[:, 0:2, :], ACT.Copy)
                        act.activation(c_hi[0:QR - P, 2, :], c_f[0:QR - P, 2, :], ACT.Copy).then_inc(s_latents_hi, 1)
                    if p == UQ_AT + 1:
                        for t in range(NT):
                            if t == 1:
                                act.wait_ge(s_panel_used, at("panel_used", l, UQ_AT + 1 + 1))
                            else:
                                act.wait_ge(s_mla_q_product, at("mla_q_product", l, 1))
                            act.activation(q_tok[:, t, :].rearrange("p (c n) -> p c n", c=2),
                                               ps[:, 4 + 2 * t:6 + 2 * t, 0:384], ACT.Copy, scale=QK ** -0.5).then_inc(s_mla_q_ready, 1)
                    if UKV_AT <= p < UKV_AT + 2:
                        c = p - UKV_AT
                        act.wait_ge(s_mla_kv_product, at("mla_kv_product", l, c + 1))
                        kd, ks, vd, vs = keys_values(c, 0)
                        act.activation(kd, ks, ACT.Copy)
                        act.activation(vd, vs, ACT.Copy).then_inc(s_mla_kv_even_ready, 1)
                    if p == Z_AT[4] + 2:
                        act.wait_ge(s_forget_logits_ready, at("forget_logits_ready", l, 1))
                        act.activation(fe[:], fe[:], ACT.Exp)
                        act.drain()
                        act.activation(fl[:], fe[:], ACT.Ln, bias=1.0).then_inc(s_forget_logs_ready, 1)
                for s in range(LAST_SLOT + 1):
                    if s % 2 == 0 and s < SLOTS:
                        split_hi(l, GATE_AT + s // 2 + 1)
                    if s < SLOTS:
                        gate(l, s)
                        head_out(l, s)
                    if s in ODD:
                        odd_out(l, s)
                    if 0 <= s - LAG_S < SLOTS:
                        softmax_exp(l, s - LAG_S)
                    if 0 <= s - SLOTS < 4:
                        split_hi(l, BR_AT + s - SLOTS + 1)
                split_hi(l, BR_AT + 5)
                split_hi(l, OUT_AT)
                for j in range(KD):
                    merged_hi(l, j)
                for q in range(4):
                    split_hi(l, OUT_AT + q + 1)
                norm(l, 0)
                x_hi(l, 1)
                for f in range(FT):
                    split_hi(l, UP_AT + f + 1)
                    if f >= 1:
                        gelu(l, f - 1, (f - 1) % 2, f < 3)
                    if f >= 2:
                        hidden_hi(l, f - 2, f % 2)
                    conv_first(l, f, f % 2)
                for p in range(DOWN_AT, NP):
                    if p < NP - 1:
                        split_hi(l, p + 1)
                    if p == DOWN_AT:
                        gelu(l, FT - 1, (FT - 1) % 2, False)
                        hidden_hi(l, FT - 2, FT % 2)
                        hidden_hi(l, FT - 1, (FT - 1) % 2)
                norm(l, 1)

        @block.vector
        def _(dve):
            def split_lo(l, p):
                dve.wait_ge(s_weights_hi, at("weights_hi", l, p + 1))
                n, ncol = panel_extent(p)
                dve.tensor_tensor(w_lo[0:n, p % 2, 0:ncol], raw[0:n, p % RAW, 0:ncol],
                                      w_hi[0:n, p % 2, 0:ncol].bitcast(F32), ALU.subtract).then_inc(s_weights_lo, 1)

            def x_lo(l, j):
                for t in range(NT):
                    dve.wait_ge(s_x_hi_ready, at("x_hi_ready", l, NT * j + t + 1))
                    tok = slice(P * t, P * t + P)
                    dve.tensor_tensor(xt_lo[:, :, tok], x_psum(t), xt_hi[:, :, tok].bitcast(F32),
                                          ALU.subtract).then_inc(s_x_lo_ready, 1)

            def z_out(l, i):
                dve.wait_ge(s_panel_used, at("panel_used", l, Z_AT[i] + 2))
                dve.tensor_copy(z1[:, 1, ZC * i:ZC * i + ZC], ps[:, B_Z[i][1], 0:ZC]).then_inc(s_z_odd_ready, 1)

            def rms_sums(l):
                dve.drain()
                dve.wait_ge(s_z_even_ready, at("z_even_ready", l, 1))
                for t in range(NT):
                    for i, (c, n) in enumerate(((C_CQ, QR), (C_CKV, KVR))):
                        z = z1[:, t, c:c + n]
                        ins = dve.tensor_tensor_reduce(cn[:, t, c:c + n], z, z, 1.0, 0.0, ALU.mult, ALU.add,
                                                       accum_out=small[:, 2 * i + t:2 * i + t + 1])
                ins.then_inc(s_latent_squares, 1)

            def rms_scale(l):
                dve.wait_ge(s_latent_rms, at("latent_rms", l, 1))
                dve.reciprocal(small[:, 8:12], small[:, 4:8])
                dve.drain()
                for t in range(NT):
                    for i, (c, n) in enumerate(((C_CQ, QR), (C_CKV, KVR))):
                        ins = dve.tensor_scalar(cn[:, t, c:c + n], z1[:, t, c:c + n],
                                                small[:, 8 + 2 * i + t:9 + 2 * i + t], None, ALU.mult)
                ins.then_inc(s_latents_normed, 1)

            def latent_gain(l):
                dve.wait_ge(s_latents_turned, at("latents_turned", l, 1))
                dve.tensor_scalar(c_f[:, 0, :], ps[:, B_LAT[0], 0:T], vec_t[:, V_QN:V_QN + 1], None, ALU.mult)
                dve.tensor_scalar(c_f[:, 1, :], ps[:, B_LAT[0], T:2 * T], vec_t[:, V_KN:V_KN + 1], None, ALU.mult)
                r = QR - P
                dve.tensor_scalar(c_f[0:r, 2, :], ps[0:r, B_LAT[1], 0:T], vec_t[0:r, V_QN + 1:V_QN + 2], None,
                                      ALU.mult).then_inc(s_latents_scaled, 1)

            def latent_lo(l):
                dve.wait_ge(s_latents_hi, at("latents_hi", l, 1))
                dve.tensor_tensor(c_lo[:, 0:2, :], c_f[:, 0:2, :], c_hi[:, 0:2, :].bitcast(F32), ALU.subtract)
                r = QR - P
                dve.tensor_tensor(c_lo[0:r, 2, :], c_f[0:r, 2, :], c_hi[0:r, 2, :].bitcast(F32),
                                      ALU.subtract).then_inc(s_latents_lo, 1)

            def rotate(first, second, c, s, tmp, out1, out2):
                for i, (a, b) in enumerate(((first, c), (second, s), (first, s), (second, c))):
                    dve.tensor_tensor(tmp[i], a, b, ALU.mult)
                dve.drain()
                dve.tensor_tensor(out1, tmp[0], tmp[1], ALU.subtract)
                return dve.tensor_tensor(out2, tmp[2], tmp[3], ALU.add)

            def rope(l):
                k1, k2 = z1[:, :, C_KR:C_KR + HALF], z1[:, :, C_KR + HALF:C_KR + ROPE]
                rotate(k1, k2, cos[:], sin[:], [krot[:, i] for i in range(4)], kr[:, :, 0:HALF], kr[:, :, HALF:])
                dve.drain()
                kt = k_tok[:].rearrange("p t (h n) -> p t h n", n=QK)
                dve.tensor_copy(kt[:, :, :, HD:QK], kr[:, :, None, :].broadcast_to([P, NT, H, ROPE]))
                dve.wait_ge(s_mla_q_ready, at("mla_q_ready", l, NT))
                qt = q_tok[:].rearrange("p t (h n) -> p t h n", n=QK)
                q1, q2 = qt[:, :, :, HD:HD + HALF], qt[:, :, :, HD + HALF:QK]
                c, s = (w[:, :, None, :].broadcast_to([P, NT, H, HALF]) for w in (cos, sin))
                rotate(q1, q2, c, s, [rot[:, i] for i in range(4)], q1, q2).then_inc(s_rotated, 1)

            def forget_logits(l):
                dve.drain()
                dve.wait_ge(s_z_even_ready, at("z_even_ready", l, 5))
                dve.tensor_tensor(fx[:], z1[:, :, C_FL:C_FL + H], bfor[:, None, :].broadcast_to([P, NT, H]), ALU.add)
                dve.drain()
                dve.scalar_tensor_tensor(fe[:], fx[:], -1.0, fx[:], ALU.mult, ALU.min).then_inc(s_forget_logits_ready, 1)

            def log_forget(l):
                dve.wait_ge(s_forget_logs_ready, at("forget_logs_ready", l, 1))
                dve.scalar_tensor_tensor(fx[:], fx[:], 0.0, fl[:], ALU.min, ALU.subtract).then_inc(s_log_forgets_ready, 1)

            def index_keys(l):
                dve.drain()
                dve.wait_ge(s_z_even_ready, at("z_even_ready", l, NZ))
                for t in range(NT):
                    ins = dve.tensor_copy(ikd[:, t, :].rearrange("p (j n) -> p j n", j=4),
                                          z1[:, t, C_IK:C_IK + IDIM][:, None, :].broadcast_to([P, 4, IDIM]))
                ins.then_inc(s_index_keys_copied, 1)

            def index_scores(l, n):
                t = 0 if n < 2 else 1
                hs = range(4 * n, 4 * n + 4) if t == 0 else range(2 * (n - 2), 2 * (n - 2) + 2)
                keys = P * (t + 1)
                dve.drain()
                dve.wait_ge(s_odd_job_read, at("odd_job_read", l, 3 + n + 1))
                for j, h in enumerate(hs):
                    w = z1[:, t, C_IW + h:C_IW + h + 1]
                    r = rel[:, n % 2, keys * j:keys * j + keys]
                    if h == 0:
                        ins = dve.tensor_scalar(ix[:, SPAN[t]], r, w, None, ALU.mult)
                    else:
                        if j:
                            dve.drain()
                        ins = dve.scalar_tensor_tensor(ix[:, SPAN[t]], r, w, ix[:, SPAN[t]], ALU.mult, ALU.add)
                ins.then_inc(s_index_head_added, 1)

            def take_eight(t):
                dve.max(top8[:], ixw[:, SPAN[t]])
                dve.drain()
                dve.match_replace(ixw[:, SPAN[t]], top8[:], ixw[:, SPAN[t]], TAKEN)
                dve.drain()

            def selection(l):
                dve.tensor_scalar(selm[:], ixw[:], (LOWEST + TAKEN) / 2, MASKED, ALU.is_gt, ALU.mult)
                dve.drain()
                dve.tensor_tensor(selm[:, 0:P], selm[:, 0:P], mask_b[:], ALU.add)
                dve.tensor_tensor(selm[:, T:3 * P], selm[:, T:3 * P], mask_b[:], ALU.add).then_inc(s_selection_ready, 1)

            def row_max(l, hh):
                b, h = divmod(hh, H)
                dve.wait_ge(s_scores_ready, at("scores_ready", l, hh + 1))
                if hh >= 2:
                    dve.wait_ge(s_probs_ready, at("probs_ready", l, hh - 1 if b < 2 else hh))
                for t in range(NT):
                    src = ps[:, B_S, SPAN[t]]
                    if b == 2:
                        dve.scalar_tensor_tensor(ssc[:, SPAN[t]], dist[:, t, 0:P * (t + 1)], -(2.0 ** -(8 * (h + 1) / H)),
                                                 src, ALU.mult, ALU.add)
                if b == 2:
                    dve.drain()
                for t in range(NT):
                    src = ssc[:, SPAN[t]] if b == 2 else ps[:, B_S, SPAN[t]]
                    ins = dve.tensor_reduce(negm[:, hh % 2, t:t + 1], src, AX.X, ALU.max, negate=True)
                ins.then_inc(s_maxima_ready, 1)

            def probs_out(l, hh):
                dve.wait_ge(s_probs_turned, at("probs_turned", l, hh + 1))
                if hh >= 2:
                    dve.wait_ge(s_head_output, at("head_output", l, hh - 1))
                dve.tensor_copy(pts[:, hh % 2, :], ps[:, B_PT, 0:3 * P]).then_inc(s_turned_probs_ready, 1)

            def normalise(l, b):
                dve.wait_ge(s_head_output, at("head_output", l, H * (b + 1)))
                if b:
                    dve.wait_ge(s_odd_product, at("odd_product", l, ODD_NO[H * b + LAG_V + 1] + 1))
                dve.reciprocal(rinv[:], rsum[:, b])
                dve.drain()
                for t in range(NT):
                    ins = dve.tensor_tensor(o_tok[:, t, :].rearrange("p (h n) -> p h n", h=H),
                                            ps[:, B_O[t], :].rearrange("p (h n) -> p h n", h=H),
                                            rinv[:, t, :][:, :, None].broadcast_to([P, H, HD]), ALU.mult)
                ins.then_inc(s_outputs_normed, 1)

            def turned_lo(l, s):
                b, t = divmod(ODD[s][1], NT)
                dve.wait_ge(s_odd_job_read, at("odd_job_read", l, ODD_NO[s] + 1))
                dst = (slice(None), slice(4 * b, 4 * b + 4), slice(P * t, P * t + P))
                dve.tensor_tensor(ot_lo[dst], ps[:, B_ODD, :].rearrange("p (k t) -> p k t", k=4),
                                      ot_hi[dst].bitcast(F32), ALU.subtract).then_inc(s_outputs_lo_ready, 1)

            def merge(l, q):
                n, c = divmod(q, 2)
                if q == 0:
                    dve.wait_ge(s_gate_ready, at("gate_ready", l, SLOTS))
                for jj in range(4):
                    j = 4 * c + jj
                    u = 8 * n + j
                    if jj == 3:
                        dve.wait_ge(s_panel_used, at("panel_used", l, BR_AT + q + 1))
                    else:
                        dve.wait_ge(s_proj_product, at("proj_product", l, 3 * q + jj + 1))
                    dst = merged[:, j, :] if n == 0 else gated[:, u % 2, :]
                    dve.scalar_tensor_tensor(dst, gates[:, u, :], 1.0, proj_psum(u), ALU.add, ALU.mult).then_inc(s_proj_gated, 1)
                    if n:
                        dve.drain()
                        ins = dve.tensor_tensor(merged[:, j, :], merged[:, j, :], dst, ALU.add)
                        if n == NB - 1:
                            ins.then_inc(s_merged_ready, 1)
                            if j:
                                merged_lo(l, j - 1)

            def merged_lo(l, j):
                dve.wait_ge(s_merged_hi_ready, at("merged_hi_ready", l, j + 1))
                dve.scalar_tensor_tensor(mg_lo[:, j, :], merged[:, j, :], 0.5, mg_hi[:, j, :].bitcast(F32),
                                             ALU.mult, ALU.subtract).then_inc(s_merged_lo_ready, 1)

            def residual(l, j, c):
                cols = slice(512 * c, 512 * c + 512)
                for t in range(NT):
                    if t == 1:
                        dve.wait_ge(s_panel_used, at("panel_used", l, (DOWN_AT + 6 * c + 5 if j else OUT_AT + 2 * c + 1) + 1))
                    else:
                        dve.wait_ge(s_residual_product, at("residual_product", l, 2 * j + c + 1))
                    dve.scalar_tensor_tensor(res[:, t, cols], x_tok[:, t, cols], ALPHA, ps[:, B_R[c][t], :],
                                             ALU.mult, ALU.add)
                    dve.drain()
                    dve.bn_stats(stats[:, t, c, :], res[:, t, cols])

            def norm(l, j):
                dve.drain()
                for t in range(NT):
                    dve.bn_aggr(mv[:, t, :], stats[:, t, :, :]).then_inc(s_variances_ready, 1)
                for t in range(NT):
                    dve.wait_ge(s_deviations_ready, at("deviations_ready", l, NT * j + t + 1))
                    dve.reciprocal(lnv[:, t, 1:2], lnv[:, t, 0:1])
                    dve.drain()
                    dve.tensor_scalar(lnv[:, t, 3:4], mv[:, t, 0:1], -1.0, lnv[:, t, 1:2], ALU.mult, ALU.mult).then_inc(s_norm_scales_ready, 1)
                for t in range(NT):
                    dve.wait_ge(s_normed_ready, at("normed_ready", l, NT * j + t + 1))
                    dve.wait_ge(s_gb, 16 * (4 * l + 2 * j + 2))
                    dve.tensor_tensor(res[:, t, :], res[:, t, :], ln_g[:], ALU.mult)
                    dve.drain()
                    dve.tensor_tensor(x_tok[:, t, :], res[:, t, :], ln_b[:], ALU.add).then_inc(s_x_ready, 1)

            def conv_rest(l, f, buf):
                dve.wait_ge(s_conv_first_tap, at("conv_first_tap", l, f + 1))
                dve.scalar_tensor_tensor(cv[:, buf, 1:T], ps[:, buf, 0:T - 1], column(vec_t, V_CW + FT, f),
                                         cv[:, buf, 1:T], ALU.mult, ALU.add)
                dve.drain()
                dve.scalar_tensor_tensor(cv[:, buf, 2:T], ps[:, buf, 0:T - 2], column(vec_t, V_CW, f),
                                             cv[:, buf, 2:T], ALU.mult, ALU.add).then_inc(s_conv_ready, 1)

            def hidden(l, f, buf, first):
                dve.wait_ge(s_gelu_ready, at("gelu_ready", l, f + 1))
                if not first:
                    dve.wait_ge(s_hidden_hi_ready, at("hidden_hi_ready", l, f - 1))
                dve.tensor_tensor(hf[:, buf, :], ge[:, buf, :], ps[:, buf, T:2 * T], ALU.mult).then_inc(s_hidden_ready, 1)

            def hidden_lo(l, f, buf):
                dve.wait_ge(s_hidden_hi_ready, at("hidden_hi_ready", l, f + 1))
                dve.tensor_tensor(tile_at(ht_lo, f), hf[:, buf, :], tile_at(ht_hi, f).bitcast(F32),
                                      ALU.subtract).then_inc(s_hidden_lo_ready, 1)

            dve.memset(vecs[:], 0.0).then_inc(s_setup, 1)
            dve.memset(group[:], 0.0)
            dve.drain()
            for j in range(4):
                dve.memset(group[IDIM * j:IDIM * j + IDIM, j:j + 1], 1.0).then_inc(s_const, 1)
            for i in range(RAW):
                dve.memset(lnv[:, 0, i:i + 1], 0.0).then_inc(s_weights_lo, 1)
            for j in range(HALF):
                dve.memset(freq[:, j:j + 1], float(inv_freq[j]))
            dve.wait_ge(s_in, 48)
            dve.tensor_copy(pos_f[:], pos_row[:])
            dve.tensor_copy(pos_c[:], pos_col[:])
            dve.drain()
            for t in range(NT):
                dve.tensor_scalar(dist[:, t, :], pos_f[:], pos_c[:, t:t + 1], None, ALU.subtract)
                dve.tensor_scalar(ang[:, t, :], freq[:], pos_c[:, t:t + 1], None, ALU.mult)
            dve.drain()
            dve.scalar_tensor_tensor(dist[:], dist[:], -1.0, dist[:], ALU.mult, ALU.max)
            dve.tensor_scalar(turns[:], ang[:], 1.0 / (2 * np.pi), ROUND, ALU.mult, ALU.add)
            dve.drain()
            dve.tensor_scalar(turns[:], turns[:], -ROUND, None, ALU.add)
            dve.drain()
            for part in TWO_PI:
                dve.scalar_tensor_tensor(ang[:], turns[:], -part, ang[:], ALU.mult, ALU.add)
                dve.drain()
            dve.tensor_scalar(angc[:], ang[:], np.pi / 2, None, ALU.add)
            dve.drain()
            dve.tensor_scalar(turns[:], angc[:], np.pi, -2 * np.pi, ALU.is_gt, ALU.mult)
            dve.drain()
            dve.tensor_tensor(angc[:], angc[:], turns[:], ALU.add)
            dve.drain()
            dve.tensor_scalar(ang[:], ang[:], PI_BELOW, -PI_BELOW, ALU.min, ALU.max)
            dve.tensor_scalar(angc[:], angc[:], PI_BELOW, -PI_BELOW, ALU.min, ALU.max).then_inc(s_setup, 1)
            for t in range(NT):
                dve.memset(eps[:, t:t + 1], (LN_EPS, RMS_EPS)[t]).then_inc(s_x_ready, 1)
            dve.wait_ge(s_trig, 1)
            dve.wait_ge(s_const, N_CONST)
            with dve.Fori(0, DEPTH) as l:
                split_lo(l, 0)
                x_lo(l, 0)
                dve.wait_ge(s_vectors_ready, at("vectors_ready", l, 1))
                dve.tensor_scalar(bg2[:], vec_t[:, V_BG:V_BG + NB * KD], 0.5, None, ALU.mult).then_inc(s_gate_bias_ready, 1)
                for p in range(GATE_AT):
                    split_lo(l, p + 1)
                    if p - 1 in Z_AT:
                        z_out(l, Z_AT.index(p - 1))
                    if p == 1:
                        rms_sums(l)
                    if p == 2:
                        rms_scale(l)
                    if p == 4:
                        latent_gain(l)
                        latent_lo(l)
                    if UKV_AT <= p < UKV_AT + 2:
                        c = p - UKV_AT
                        dve.wait_ge(s_panel_used, at("panel_used", l, p + 1))
                        kd, ks, vd, vs = keys_values(c, 1)
                        dve.tensor_copy(kd, ks)
                        dve.tensor_copy(vd, vs).then_inc(s_mla_kv_odd_ready, 1)
                    if p == UKV_AT + 1:
                        rope(l)
                    if p == Z_AT[4] + 1:
                        forget_logits(l)
                    if p == Z_AT[4] + 2:
                        log_forget(l)
                index_keys(l)
                for s in range(LAST_SLOT + 1):
                    if s % 2 == 0 and s < SLOTS:
                        split_lo(l, GATE_AT + s // 2 + 1)
                    if s == 6:
                        dve.wait_ge(s_index_masked, at("index_masked", l, 1))
                    if s == 10:
                        dve.wait_ge(s_index_masked, at("index_masked", l, 2))
                    if s in ODD and ODD[s][0] == "turn":
                        turned_lo(l, s)
                    if 0 <= s - LAG_S < SLOTS:
                        row_max(l, s - LAG_S)
                    if 0 <= s - LAG_T < SLOTS:
                        probs_out(l, s - LAG_T)
                    if s - 4 in range(6):
                        index_scores(l, s - 4)
                    if 6 <= s < 14:
                        for _ in range(TOPK // 8 // 4):
                            take_eight(0 if s < 10 else 1)
                    if s == 14:
                        selection(l)
                    if s >= H + 2 and (s - H - 2) % H == 0:
                        normalise(l, (s - H - 2) // H)
                    if 0 <= s - SLOTS < 4:
                        split_lo(l, BR_AT + s - SLOTS + 1)
                        merge(l, s - SLOTS)
                for q in (4, 5):
                    split_lo(l, BR_AT + q + 1)
                    merge(l, q)
                merged_lo(l, KD - 1)
                for q in range(4):
                    split_lo(l, OUT_AT + q + 1)
                    if q % 2:
                        residual(l, 0, q // 2)
                norm(l, 0)
                x_lo(l, 1)
                for f in range(FT):
                    split_lo(l, UP_AT + f + 1)
                    if f >= 1:
                        hidden(l, f - 1, (f - 1) % 2, f < 3)
                    if f >= 2:
                        hidden_lo(l, f - 2, f % 2)
                    conv_rest(l, f, f % 2)
                for p in range(DOWN_AT, NP):
                    if p < NP - 1:
                        split_lo(l, p + 1)
                    if p == DOWN_AT:
                        hidden(l, FT - 1, (FT - 1) % 2, False)
                        hidden_lo(l, FT - 2, FT % 2)
                        hidden_lo(l, FT - 1, (FT - 1) % 2)
                    if (p - DOWN_AT) % 6 == 5:
                        residual(l, 1, (p - DOWN_AT) // 6)
                norm(l, 1)

        @block.gpsimd
        def _(pool):
            pool.memset(ident[:], 0.0)
            pool.memset(mask_b[:], 0.0)
            pool.memset(tri[:], 1.0).then_inc(s_pool, 1)
            pool.wait_ge(s_pool, 1)
            pool.affine_select(out=ident[:], in_=ident[:], compare_op=ALU.not_equal, fill=1.0, base=0,
                               pattern=[[-1, P]], channel_multiplier=1).then_inc(s_pool, 1)
            pool.affine_select(out=mask_b[:], in_=mask_b[:], compare_op=ALU.is_ge, fill=MASKED, base=0,
                               pattern=[[-1, P]], channel_multiplier=1).then_inc(s_const, 1)
            pool.affine_select(out=tri[:, 0:P], in_=tri[:, 0:P], compare_op=ALU.is_ge, fill=0.0, base=0,
                               pattern=[[1, P]], channel_multiplier=-1).then_inc(s_const, 1)
            pool.wait_ge(s_pool, 2)
            pool.tensor_copy(ident_b[:], ident[:]).then_inc(s_const, 1)
            def take_wait():
                pool.tensor_tensor(waited[:], group[:, 0:1], group[:, 0:1], ALU.mult)

            pool.wait_ge(s_const, N_CONST)
            with pool.Fori(0, DEPTH) as l:
                pool.wait_ge(s_z_even_ready, at("z_even_ready", l, 3))
                pool.wait_ge(s_z_odd_ready, at("z_odd_ready", l, 3))
                take_wait()
                for t in range(NT):
                    for dst, c, scale in ((fq_aug, C_FQ, HD ** -0.5), (fk_aug, C_FK, 1.0)):
                        pool.tensor_scalar(dst[:, t, :, 0:HD], z1[:, t, c:c + H * HD].rearrange("p (h n) -> p h n", h=H),
                                           scale, None, ALU.mult)
                pool.memset(fq_aug[:, :, :, HD + 1], 1.0)
                pool.memset(fk_aug[:, :, :, HD], 1.0).then_inc(s_decay_operands_ready, 1)
                pool.wait_ge(s_index_head_added, at("index_head_added", l, 2))
                take_wait()
                pool.affine_select(out=ixw[:, SPAN[0]], in_=ix[:, SPAN[0]], compare_op=ALU.is_ge, fill=LOWEST,
                                       base=0, pattern=[[-1, P]], channel_multiplier=1).then_inc(s_index_masked, 1)
                pool.wait_ge(s_index_head_added, at("index_head_added", l, 6))
                take_wait()
                pool.affine_select(out=ixw[:, SPAN[1]], in_=ix[:, SPAN[1]], compare_op=ALU.is_ge, fill=LOWEST,
                                       base=P, pattern=[[-1, T]], channel_multiplier=1).then_inc(s_index_masked, 1)

    return nc


_ARGS = ["x", "positions", "w_in", "b_gate", "b_forget", "mla_q_norm", "mla_kv_norm", "mla_w_uq", "mla_w_ukv",
         "w_branch", "w_out", "ln1_g", "ln1_b", "ffn_w_up", "ffn_conv_w", "ffn_conv_b", "ffn_w_down", "ln2_g", "ln2_b"]


def kernel(**inputs):
    import concourse.bacc as bacc
    from concourse.bass_utils import run_bass_kernel_spmd

    nc = bacc.Bacc("TRN2", target_bir_lowering=False, num_devices=1)
    arrays = {n: np.ascontiguousarray(inputs[n]) for n in _ARGS}
    args = [nc.dram_tensor(n, a.shape, mybir.dt.from_np(a.dtype), kind="ExternalInput").ap() for n, a in arrays.items()]
    out = nc.dram_tensor("out", arrays["x"].shape, F32, kind="ExternalOutput").ap()
    build_program(nc, *args, out)
    return run_bass_kernel_spmd(nc, [arrays], core_ids=[0]).results[0]["out"]
```

```python
from contextlib import ExitStack

import numpy as np

import concourse.bass as bass
from concourse import mybir

F32 = mybir.dt.float32
F32R = mybir.dt.float32r
BF16 = mybir.dt.bfloat16
I32 = mybir.dt.int32
ACT = mybir.ActivationFunctionType
ALU = mybir.AluOpType
AX = mybir.AxisListType

P = 128
T = 256
NT = T // P
DM = 1024
KD = DM // P
H = 8
NB = 3
HD = 64
ROPE = 32
HALF = ROPE // 2
QK = HD + ROPE
QR = 192
KVR = 128
IH, IDIM = 8, 32
DFF = 2816
FT = DFF // P
TOPK = T // 4
DEPTH = 2
ALPHA = float((2 * DEPTH) ** 0.25)
LN_EPS, RMS_EPS = 1e-5, 1e-6
THETA = 10000.0

WIDTHS = (QR, KVR, ROPE, H * HD, H * HD, H * HD, H, H * HD, HD, HD, IH * IDIM, IDIM, IH, NB * DM)
OFFS = [sum(WIDTHS[:i]) for i in range(len(WIDTHS) + 1)]
(C_CQ, C_CKV, C_KR, C_FQ, C_FK, C_FV, C_FL, C_SQ, C_SK, C_SV, C_IQ, C_IK, C_IW, C_GATE, DIN) = OFFS
ZW = C_GATE
NZ = 6
ZC = ZW // NZ

PANEL = 2048
Z_AT = [(0, 1), (2, 3), (4, 5), (6, 8), (9, 11), (12, 13)]
UQ_AT, UKV_AT = 7, 10
Z_LAST = [b for _, b in Z_AT]
GATE_AT = 14
BR_AT = GATE_AT + NB * KD // 2
OUT_AT = BR_AT + 2 * NB
UP_AT = OUT_AT + 4
DOWN_AT = UP_AT + FT
DOWN_K = [4, 3, 3, 3, 3, 3, 3]
NP = DOWN_AT + 2 * len(DOWN_K)
NGATED = 4
RAW = 3
assert NP % 2 == 0 and NP % RAW == 0

MASKED = -1e30
LOWEST = -3.0e38
TAKEN = -3.3e38
SLOTS = NB * H
LAG_S, LAG_T, LAG_V = 1, 2, 3

ODD = {0: ("iq", 0), 1: ("ik", 0), 2: ("cum", 0)}
ODD.update({3 + n: ("index", n) for n in range(6)})
ODD.update({H * (b + 1) + LAG_V + (b < NB - 1) + t: ("turn", NT * b + t) for b in range(NB) for t in range(NT)})
ODD_ORDER = sorted(ODD)
ODD_NO = {s: i for i, s in enumerate(ODD_ORDER)}
N_ODD = len(ODD)
LAST_SLOT = SLOTS + LAG_V

B_GATE, B_S, B_PT, B_QK, B_ODD, B_O = (0, 1), 2, 3, 4, 5, (6, 7)
B_PROJ = [(0, 1, 4)[u % 3] for u in range(KD)] + [(2, 3, 0, 1, 4)[u % 5] for u in range((NB - 1) * KD)]
B_PROJ[-1] = B_ODD
B_R = ((2, 3), (0, 1))
B_X = ((4, 5), (6, 7))
B_LAT = (4, 5)
B_Z = ((0, 1), (2, 3), (0, 1), (2, 3), (0, 1), (6, 7))
B_KV = ((2, 3), (4, 5))

PER = dict(
    weights_hi=NP, weights_lo=NP, first_half_split=1, panel_used=NP,
    x_ready_0=4, x_ready_1=4, x_turned=4 * NT, x_hi_ready=4 * NT, x_lo_ready=4 * NT,
    vectors_turned=1, vectors_ready=1, gate_bias_ready=1,
    z_product=NZ, z_even_ready=NZ, z_odd_ready=NZ,
    latent_squares=1, latent_rms=1, latents_normed=1, latents_turned=1, latents_scaled=1, latents_hi=1, latents_lo=1,
    mla_q_product=1, mla_q_ready=NT, rotations_ready=1, rotated=1, mla_kv_product=3, mla_kv_even_ready=2,
    mla_kv_odd_ready=2,
    forget_logits_ready=1, forget_logs_ready=1, log_forgets_ready=1, index_keys_copied=1, decay_operands_ready=1,
    gate_product=SLOTS // 2, gate_ready=SLOTS, head_turned=SLOTS, head_ready=SLOTS,
    scores_ready=SLOTS, maxima_ready=SLOTS, probs_ready=SLOTS, probs_turned=SLOTS, turned_probs_ready=SLOTS,
    head_output=SLOTS, outputs_normed=NB,
    odd_product=N_ODD, odd_job_read=N_ODD, outputs_lo_ready=NB * NT, index_head_added=6, index_masked=NT,
    selection_ready=1,
    proj_product=NB * KD * 3 // 4, proj_gated=NB * KD, merged_added=(NB - 1) * KD, merged_hi_ready=KD,
    merged_lo_ready=KD,
    residual_product=4, variances_ready=2 * NT, deviations_ready=2 * NT, centred=2, scaled=4,
    conv_first_tap=FT, conv_ready=FT, gelu_ready=FT, hidden_ready=FT, hidden_hi_ready=FT, hidden_lo_ready=FT,
)


def build_program(nc, x, positions, w_in, b_gate, b_forget, q_norm, kv_norm, w_uq, w_ukv, w_branch, w_out,
                  ln1_g, ln1_b, w_up, conv_w, conv_b, w_down, ln2_g, ln2_b, out):
    ctx = ExitStack()
    with ctx:
        def sb(name, shape, dt=F32):
            return ctx.enter_context(nc.sbuf_tensor(name, shape, dt))

        def sem(name):
            return ctx.enter_context(nc.semaphore(name))

        s_weights_hi = sem("weights_hi")
        s_weights_lo = sem("weights_lo")
        s_first_half_split = sem("first_half_split")
        s_panel_used = sem("panel_used")
        s_x_ready_0 = sem("x_ready_0")
        s_x_ready_1 = sem("x_ready_1")
        s_x_turned = sem("x_turned")
        s_x_hi_ready = sem("x_hi_ready")
        s_x_lo_ready = sem("x_lo_ready")
        s_vectors_turned = sem("vectors_turned")
        s_vectors_ready = sem("vectors_ready")
        s_gate_bias_ready = sem("gate_bias_ready")
        s_z_product = sem("z_product")
        s_z_even_ready = sem("z_even_ready")
        s_z_odd_ready = sem("z_odd_ready")
        s_latent_squares = sem("latent_squares")
        s_latent_rms = sem("latent_rms")
        s_latents_normed = sem("latents_normed")
        s_latents_turned = sem("latents_turned")
        s_latents_scaled = sem("latents_scaled")
        s_latents_hi = sem("latents_hi")
        s_latents_lo = sem("latents_lo")
        s_mla_q_product = sem("mla_q_product")
        s_mla_q_ready = sem("mla_q_ready")
        s_rotations_ready = sem("rotations_ready")
        s_rotated = sem("rotated")
        s_mla_kv_product = sem("mla_kv_product")
        s_mla_kv_even_ready = sem("mla_kv_even_ready")
        s_mla_kv_odd_ready = sem("mla_kv_odd_ready")
        s_forget_logits_ready = sem("forget_logits_ready")
        s_forget_logs_ready = sem("forget_logs_ready")
        s_log_forgets_ready = sem("log_forgets_ready")
        s_index_keys_copied = sem("index_keys_copied")
        s_decay_operands_ready = sem("decay_operands_ready")
        s_gate_product = sem("gate_product")
        s_gate_ready = sem("gate_ready")
        s_head_turned = sem("head_turned")
        s_head_ready = sem("head_ready")
        s_scores_ready = sem("scores_ready")
        s_maxima_ready = sem("maxima_ready")
        s_probs_ready = sem("probs_ready")
        s_probs_turned = sem("probs_turned")
        s_turned_probs_ready = sem("turned_probs_ready")
        s_head_output = sem("head_output")
        s_outputs_normed = sem("outputs_normed")
        s_odd_product = sem("odd_product")
        s_odd_job_read = sem("odd_job_read")
        s_outputs_lo_ready = sem("outputs_lo_ready")
        s_index_head_added = sem("index_head_added")
        s_index_masked = sem("index_masked")
        s_selection_ready = sem("selection_ready")
        s_proj_product = sem("proj_product")
        s_proj_gated = sem("proj_gated")
        s_merged_added = sem("merged_added")
        s_merged_hi_ready = sem("merged_hi_ready")
        s_merged_lo_ready = sem("merged_lo_ready")
        s_residual_product = sem("residual_product")
        s_variances_ready = sem("variances_ready")
        s_deviations_ready = sem("deviations_ready")
        s_centred = sem("centred")
        s_scaled = sem("scaled")
        s_conv_first_tap = sem("conv_first_tap")
        s_conv_ready = sem("conv_ready")
        s_gelu_ready = sem("gelu_ready")
        s_hidden_ready = sem("hidden_ready")
        s_hidden_hi_ready = sem("hidden_hi_ready")
        s_hidden_lo_ready = sem("hidden_lo_ready")
        loaded = [ctx.enter_context(nc.semaphore(f"w_loaded{i}")) for i in range(RAW)]
        s_in = ctx.enter_context(nc.semaphore("inputs_loaded"))
        s_x_in = [ctx.enter_context(nc.semaphore(f"x_loaded{t}")) for t in range(NT)]
        s_vecs = ctx.enter_context(nc.semaphore("vectors_loaded"))
        s_gb = ctx.enter_context(nc.semaphore("norm_vectors_loaded"))
        s_const = ctx.enter_context(nc.semaphore("constants_ready"))
        s_setup = ctx.enter_context(nc.semaphore("setup_steps"))
        s_out = ctx.enter_context(nc.semaphore("outputs_stored"))
        BEFORE = dict(weights_lo=RAW)

        def at(name, l, count):
            return l * PER[name] + count + BEFORE.get(name, 0)

        ps = ctx.enter_context(nc.psum_tensor("ps", [P, 8, 512], F32))

        raw = sb("raw", [P, RAW, PANEL])
        w_hi = sb("w_hi", [P, 2, PANEL], F32R)
        w_lo = sb("w_lo", [P, 2, PANEL], F32R)
        x_tok = sb("x_tok", [P, NT, DM])
        xt_hi = sb("xt_hi", [P, KD, T], F32R)
        xt_lo = sb("xt_lo", [P, KD, T], F32R)
        ident = sb("ident", [P, P])
        ident_b = sb("ident_b", [P, P], BF16)
        mask_b = sb("mask_b", [P, P], BF16)
        tri = sb("tri", [P, T])
        dist = sb("dist", [P, NT, T])
        cos = sb("cos_t", [P, NT, HALF])
        sin = sb("sin_t", [P, NT, HALF])
        ang = sb("ang", [P, NT, HALF])
        angc = sb("angc", [P, NT, HALF])
        vecs = sb("vecs", [P, P])
        vec_t = sb("vec_t", [P, P])
        bg2 = sb("bg2", [P, NB * KD])
        bfor = sb("bfor", [P, H])
        eps = sb("eps", [P, 2])
        ot_hi = sb("ot_hi", [P, NB * 4, T], F32R)
        ot_lo = sb("ot_lo", [P, NB * 4, T], F32R)
        group = sb("group", [P, 4])
        waited = sb("waited", [P, 1])
        V_CW, V_CB, V_BG = 0, 3 * FT, 4 * FT
        V_QN = V_BG + NB * KD
        V_KN = V_QN + 2
        V_END = V_KN + 1

        def sized(stack):
            return lambda name, shape, dt=F32: stack.enter_context(nc.sbuf_tensor(name, shape, dt))

        with ExitStack() as over:
            so = sized(over)
            mg_hi = so("mg_hi", [P, KD, T], F32R)
            mg_lo = so("mg_lo", [P, KD, T], F32R)

        with ExitStack() as att:
            sa = sized(att)
            z1 = sa("z1", [P, NT, ZW])
            gates = sa("gates", [P, NB * KD, T])
            with ExitStack() as over:
                so = sized(over)
                merged = so("merged", [P, KD, T])
                gated = so("gated", [P, NGATED, T])
            q_tok = sa("q_tok", [P, NT, H * QK])
            k_tok = sa("k_tok", [P, NT, H * QK])
            with ExitStack() as over:
                so = sized(over)
                o_tok = so("o_tok", [P, NT, H * HD])
            v_tok = sa("v_tok", [P, NT, H * HD])
            fq_aug = sa("fq_aug", [P, NT, H, HD + 2])
            fk_aug = sa("fk_aug", [P, NT, H, HD + 2])
            rsum = sa("rsum", [P, NB, NT, H])
            rinv = sa("rinv", [P, NT, H])
            small = sa("small", [P, 16])
            fx = sa("fx", [P, NT, H])
            fe = sa("fe", [P, NT, H])
            fl = sa("fl", [P, NT, H])
            with ExitStack() as lat:
                sl = sized(lat)
                c_f = sl("c_f", [P, 3, T])
                c_hi = sl("c_hi", [P, 3, T], F32R)
                c_lo = sl("c_lo", [P, 3, T], F32R)
                cn = sl("cn", [P, NT, QR + KVR])
                rot = sl("rot", [P, 4, NT, H, HALF])
                krot = sl("krot", [P, 4, NT, HALF])
                kr = sl("kr", [P, NT, ROPE])
            with ExitStack() as heads:
                sh = sized(heads)
                qks = sh("qks", [P, 2, 2, T])
                prob = sh("prob", [P, 2, 3 * P])
                pts = sh("pts", [P, 2, 3 * P])
                ikd = sh("ikd", [P, NT, P])
                iqt = sh("iqt", [P, 2, T])
                ikt = sh("ikt", [P, 4, T])
                skt = sh("skt", [HD, T])
                rel = sh("rel", [P, 2, 512])
                with ExitStack() as over:
                    ssc = sized(over)("ssc", [P, 3 * P])
                ix = sh("ix", [P, 3 * P])
                ixw = sh("ixw", [P, 3 * P])
                top8 = sh("top8", [P, 8])
                selm = sh("selm", [P, 3 * P], BF16)
                negm = sh("negm", [P, 2, NT])

        with ExitStack() as ffn:
            sf = sized(ffn)
            ht_hi = sf("ht_hi", [P, FT, T], F32R)
            ht_lo = sf("ht_lo", [P, FT, T], F32R)
            cv = sf("cv", [P, 2, T])
            ge = sf("ge", [P, 2, T])
            hf = sf("hf", [P, 2, T])
            res = sf("res", [P, NT, DM])
            ln_g = sf("ln_g", [P, DM])
            ln_b = sf("ln_b", [P, DM])
            stats = sf("stats", [P, NT, 2, 6])
            mv = sf("mv", [P, NT, 2])
            dev = sf("dev", [P, NT])
            rdev = sf("rdev", [P, NT])
            scratch = sf("scratch", [P, 4])

        with ExitStack() as start:
            ss = sized(start)
            pos_row = ss("pos_row", [P, T], I32)
            pos_col = ss("pos_col", [P, NT], I32)
            pos_f = ss("pos_f", [P, T])
            pos_c = ss("pos_c", [P, NT])
            freq = ss("freq", [P, HALF])
            turns = ss("turns", [P, NT, HALF])


        SPAN = (slice(0, P), slice(P, 3 * P))
        HEAD_ROWS = (QK, HD + 2, HD)
        ROUND = 1.5 * 2 ** 23
        TWO_PI = (6.28125, 0.0019340515136718750, float(np.float32(2 * np.pi - 6.28125 - 0.0019340515136718750)))
        PI_BELOW = 3.1415925
        N_CONST = 7
        N_VECS = 7
        s_pool = ctx.enter_context(nc.semaphore("gpsimd_constants"))

        def column(w, c0, f):
            return w[:, c0 + f:c0 + f + 1] if isinstance(f, int) else w[:, bass.ds(f + c0, 1)]

        def tile_at(w, f):
            return w[:, f, :] if isinstance(f, int) else w[:, bass.ds(f, 1), :].rearrange("p a t -> p (a t)")

        def odd_jobs(s):
            return [job for job in ODD_ORDER if min(job, LAST_SLOT) == s]

        def odd_psum(job):
            return ps[:, B_O[0] if job == ODD_ORDER[-1] else B_ODD, :]

        def x_half(t, half):
            k = KD // 2
            return ((slice(None), slice(k * half, k * half + k), slice(P * t, P * t + P)),
                    ps[:, B_X[t][half], :].rearrange("p (k t) -> p k t", t=P))

        def keys_values(c, t):
            src = ps[:, B_KV[c][t], :].rearrange("p (h n) -> p h n", n=2 * HD)
            k = k_tok[:, t, 4 * QK * c:4 * QK * (c + 1)].rearrange("p (h n) -> p h n", n=QK)
            v = v_tok[:, t, 4 * HD * c:4 * HD * (c + 1)].rearrange("p (h n) -> p h n", n=HD)
            return k[:, :, 0:HD], src[:, :, 0:HD], v, src[:, :, HD:2 * HD]

        def proj_psum(u):
            return ps[:, B_PROJ[u], 0:T]

        inv_freq = (np.float32(THETA) ** (-np.arange(HALF, dtype=np.float32) / np.float32(HALF))).astype(np.float32)

        def loaded_count(l, p):
            return 32 * (l * (NP // RAW) + p // RAW + 1)

        def weight_rows(w, l, r0, nr, c0, ncol):
            return w[bass.ds(l, 1), r0:r0 + nr, c0:c0 + ncol].rearrange("a (k p) n -> p (a k) n", p=P)

        def view(buf, slot, k, ncol, k0=0, nk=None):
            nk = k - k0 if nk is None else nk
            return buf[:, slot, 0:k * ncol].rearrange("p (k n) -> p k n", k=k)[:, k0:k0 + nk, :]

        def halves(l, p):
            s = p % RAW

            def cut(w, r0, k, c0, ncol):
                a = k // 2
                return [(view(raw, s, k, ncol, 0, a), weight_rows(w, l, r0, a * P, c0, ncol)),
                        (view(raw, s, k, ncol, a), weight_rows(w, l, r0 + a * P, (k - a) * P, c0, ncol))]

            for i, at in enumerate(Z_AT):
                if p in at:
                    return cut(w_in, 512 * at.index(p), 4, ZC * i, ZC)
            if p == UQ_AT:
                return [(raw[0:n, s, c:c + H * QK],
                         w_uq[bass.ds(l, 1), r:r + n, :].rearrange("a p n -> p (a n)"))
                        for n, r, c in ((P, 0, 0), (QR - P, P, H * QK))]
            if p == UKV_AT:
                return [(raw[:, s, c:c + 512],
                         w_ukv[bass.ds(l, 1), :, c:c + 512].rearrange("a p n -> p (a n)")) for c in (0, 512)]
            if p < BR_AT:
                return cut(w_in, 0, KD, C_GATE + T * (p - GATE_AT), 256)
            if p < OUT_AT:
                n, c = divmod(p - BR_AT, 2)
                wb = w_branch[bass.ds(l, 1), n].rearrange("a k n -> a k n")
                return [(view(raw, s, 4, 512, 2 * i, 2),
                         wb[:, 256 * i:256 * i + 256, 512 * c:512 * c + 512].rearrange("a (k p) n -> p (a k) n", p=P))
                        for i in range(2)]
            if p < UP_AT:
                c, kh = divmod(p - OUT_AT, 2)
                return cut(w_out, 512 * kh, 4, 512 * c, 512)
            if p < DOWN_AT:
                return up_halves(l, s, p - UP_AT)
            c, g = divmod(p - DOWN_AT, len(DOWN_K))
            return cut(w_down, P * sum(DOWN_K[:g]), DOWN_K[g], 512 * c, 512)

        def up_halves(l, s, f):
            return [(view(raw, s, KD, 2 * P)[:, :, P * i:P * i + P],
                     w_up[bass.ds(l, 1), :, bass.ds(f * P + DFF * i, P)].rearrange("a (k p) n -> p (a k) n", p=P))
                    for i in range(2)]

        def panel_extents(p):
            if any(p in at for at in Z_AT):
                return [(P, slice(0, 4 * ZC))]
            if p == UQ_AT:
                return [(P, slice(0, H * QK)), (QR - P, slice(H * QK, 2 * H * QK))]
            if p == UKV_AT:
                return [(P, slice(0, 1024))]
            if p >= DOWN_AT:
                return [(P, slice(0, 512 * DOWN_K[(p - DOWN_AT) % len(DOWN_K)]))]
            return [(P, slice(0, PANEL))]

        FIRST_COLS = [slice(0, 2 * ZC), slice(2 * ZC, 3 * ZC), slice(3 * ZC, 4 * ZC)]

        block = ctx.enter_context(nc.Block())

        @block.sync
        def _(sp):
            for t in range(NT):
                sp.dma_start(x_tok[:, t, :], x[0, P * t:P * t + P, :]).then_inc(s_x_in[t], 16)
            with sp.Fori(0, DEPTH) as l:
                for p in range(NP):
                    sp.wait_ge(s_weights_lo, at("weights_lo", l, p - RAW + 1))
                    for dst, src in halves(l, p):
                        sp.dma_start(dst, src).then_inc(loaded[p % RAW], 16)
            for t in range(NT):
                for half in range(2):
                    cols = slice(512 * half, 512 * half + 512)
                    if t == 0:
                        sp.wait_ge(s_x_ready_0, DEPTH * PER["x_ready_0"] + half + 1)
                    else:
                        sp.wait_ge(s_x_ready_1, DEPTH * PER["x_ready_1"] + half + 1)
                    sp.dma_start(out[0, P * t:P * t + P, cols], x_tok[:, t, cols]).then_inc(s_out, 16)
            sp.wait_ge(s_out, 16 * 2 * NT)

        @block.tensor
        def _(pe):
            def product(dst, a_hi, a_lo, b_hi, b_lo, first, last):
                pe.matmul(dst, a_hi, b_hi, start=first, stop=False)
                pe.matmul(dst, a_hi, b_lo, start=False, stop=False)
                return pe.matmul(dst, a_lo, b_hi, start=False, stop=last)

            def panel(l, p, k, ncol):
                pe.wait_ge(s_weights_lo, at("weights_lo", l, p + 1))
                return view(w_hi, p % 2, k, ncol), view(w_lo, p % 2, k, ncol)

            def by_token(l, p, k_of, nk, ncol, lhs, banks, first, last):
                whi, wlo = panel(l, p, nk, ncol)
                for t in range(NT):
                    tok = slice(P * t, P * t + P)
                    for k in range(nk):
                        kk = k_of + k
                        ins = product(ps[:, banks[t], 0:ncol], lhs[0][:, kk, tok], lhs[1][:, kk, tok],
                                      whi[:, k, :], wlo[:, k, :], first and k == 0, last and k == nk - 1)
                    yield t, ins

            def last_two_panels(l, p, k_of, nk, lhs, first):
                steps = [(0, 0, k) for k in range(nk[0])] + [(1, 0, k) for k in range(2)]
                steps += [(0, 1, k) for k in range(nk[1])]
                steps += [(1, 0, k) for k in range(2, nk[0])] + [(1, 1, k) for k in range(nk[1])]
                for t, i, k in steps:
                    if t == 0 and k == 0:
                        pe.wait_ge(s_weights_lo, at("weights_lo", l, p + i + 1))
                    tok = slice(P * t, P * t + P)
                    whi, wlo = view(w_hi, (p + i) % 2, nk[i], 512), view(w_lo, (p + i) % 2, nk[i], 512)
                    ins = product(ps[:, B_R[1][t], :], lhs[0][:, k_of[i] + k, tok], lhs[1][:, k_of[i] + k, tok],
                                  whi[:, k, :], wlo[:, k, :], first and i == 0 and k == 0, i == 1 and k == nk[i] - 1)
                    if k == nk[i] - 1 and t == 1:
                        ins.then_inc(s_panel_used, 1)
                    elif k == nk[i] - 1 and i == 1:
                        ins.then_inc(s_residual_product, 1)

            def keep_clock_up(bank, n):
                for _ in range(n):
                    pe.transpose(ps[:, bank, 0:P], ident[:], ident[:])

            def turn_x(l, j):
                keep_clock_up(B_X[1][1], 6)
                for t in range(NT):
                    for half in range(2):
                        if t == 0:
                            pe.wait_ge(s_x_ready_0, at("x_ready_0", l, 2 * j + half + 1))
                        else:
                            pe.wait_ge(s_x_ready_1, at("x_ready_1", l, 2 * j + half + 1))
                        for k in range(KD // 2):
                            kk = KD // 2 * half + k
                            ins = pe.transpose(ps[:, B_X[t][half], P * k:P * k + P], x_tok[:, t, P * kk:P * kk + P],
                                               ident[:])
                        ins.then_inc(s_x_turned, 1)

            def z_panel(l, i, half):
                if half == 0 and 2 <= i <= 4:
                    pe.wait_ge(s_z_even_ready, at("z_even_ready", l, i - 1))
                    pe.wait_ge(s_z_odd_ready, at("z_odd_ready", l, i - 1))
                if half == 0 and i == 5:
                    pe.wait_ge(s_mla_q_ready, at("mla_q_ready", l, NT))
                p = Z_AT[i][half]
                for t, ins in by_token(l, p, 4 * half, 4, ZC, (xt_hi, xt_lo), B_Z[i], half == 0, half == 1):
                    if half == 1 and t == 0:
                        ins.then_inc(s_z_product, 1)
                ins.then_inc(s_panel_used, 1)

            def latents(l):
                pe.wait_ge(s_latents_normed, at("latents_normed", l, 1))
                for t in range(NT):
                    pe.transpose(ps[:, B_LAT[0], P * t:P * t + P], cn[:, t, 0:P], ident[:])
                    pe.transpose(ps[:, B_LAT[0], T + P * t:T + P * t + P], cn[:, t, QR:QR + KVR], ident[:])
                    ins = pe.transpose(ps[0:QR - P, B_LAT[1], P * t:P * t + P], cn[:, t, P:QR], ident[:])
                ins.then_inc(s_latents_turned, 1)

            def mla_queries(l):
                p, s = UQ_AT, UQ_AT % 2
                pe.wait_ge(s_latents_lo, at("latents_lo", l, 1))
                pe.wait_ge(s_weights_lo, at("weights_lo", l, p + 1))
                for t in range(NT):
                    tok = slice(P * t, P * t + P)
                    for c in range(2):
                        for half, (n, kk) in enumerate(((P, 0), (QR - P, 2))):
                            cols = slice(H * QK * half + 384 * c, H * QK * half + 384 * c + 384)
                            ins = product(ps[:, 4 + 2 * t + c, 0:384], c_hi[0:n, kk, tok], c_lo[0:n, kk, tok],
                                          w_hi[0:n, s, cols], w_lo[0:n, s, cols], half == 0, half == 1)
                    if t == 0:
                        ins.then_inc(s_mla_q_product, 1)
                ins.then_inc(s_panel_used, 1)

            def mla_keys(l):
                p = UKV_AT
                pe.wait_ge(s_z_even_ready, at("z_even_ready", l, 4))
                pe.wait_ge(s_z_odd_ready, at("z_odd_ready", l, 4))
                pe.wait_ge(s_weights_lo, at("weights_lo", l, p + 1))
                for c in range(2):
                    if c == 1:
                        pe.wait_ge(s_mla_q_ready, at("mla_q_ready", l, 1))
                    for t in range(NT):
                        tok = slice(P * t, P * t + P)
                        cols = slice(512 * c, 512 * c + 512)
                        ins = product(ps[:, B_KV[c][t], :], c_hi[:, 1, tok], c_lo[:, 1, tok],
                                      w_hi[:, p % 2, cols], w_lo[:, p % 2, cols], True, True)
                        if c == 0 or t == 0:
                            ins.then_inc(s_mla_kv_product, 1)
                ins.then_inc(s_panel_used, 1)

            def gate_tile(l, s):
                p = GATE_AT + s // 2
                if s % 2 == 0:
                    pe.wait_ge(s_weights_lo, at("weights_lo", l, p + 1))
                if s == 0:
                    pe.wait_ge(s_z_even_ready, at("z_even_ready", l, 5))
                    pe.wait_ge(s_z_odd_ready, at("z_odd_ready", l, 5))
                if s >= 2:
                    pe.wait_ge(s_gate_ready, at("gate_ready", l, s - 1))
                whi, wlo = view(w_hi, p % 2, KD, T), view(w_lo, p % 2, KD, T)
                cols = slice(P * (s % 2), P * (s % 2) + P)
                for k in range(KD):
                    ins = product(ps[:, B_GATE[s % 2], 0:T], whi[:, k, cols], wlo[:, k, cols],
                                  xt_hi[:, k, :], xt_lo[:, k, :], k == 0, k == KD - 1)
                if s % 2:
                    ins.then_inc(s_panel_used, 1)
                else:
                    ins.then_inc(s_gate_product, 1)

            def head_operands_ready(l, s):
                if s == 0:
                    pe.wait_ge(s_rotated, at("rotated", l, 1))
                    pe.wait_ge(s_mla_kv_even_ready, at("mla_kv_even_ready", l, 2))
                    pe.wait_ge(s_mla_kv_odd_ready, at("mla_kv_odd_ready", l, 2))
                else:
                    pe.wait_ge(s_head_ready, at("head_ready", l, s))
                if s == H:
                    pe.wait_ge(s_decay_operands_ready, at("decay_operands_ready", l, 1))
                    pe.wait_ge(s_odd_job_read, at("odd_job_read", l, ODD_NO[2] + 1))
                if s == 2 * H:
                    pe.wait_ge(s_z_even_ready, at("z_even_ready", l, NZ))
                    pe.wait_ge(s_z_odd_ready, at("z_odd_ready", l, NZ))

            def head_operands(l, s):
                b, h = divmod(s, H)
                for t in range(NT):
                    if b == 0:
                        q, k = (w[:, t, QK * h:QK * h + QK] for w in (q_tok, k_tok))
                    elif b == 1:
                        q, k = fq_aug[:, t, h, :], fk_aug[:, t, h, :]
                    else:
                        q, k = z1[:, t, C_SQ + HD * h:C_SQ + HD * h + HD], None
                    d = HEAD_ROWS[b]
                    ins = pe.transpose(ps[0:d, B_QK, P * t:P * t + P], q, ident[:])
                    if k is not None:
                        ins = pe.transpose(ps[0:d, B_QK, T + P * t:T + P * t + P], k, ident[:])
                ins.then_inc(s_head_turned, 1)

            def odd_job(l, s):
                what, n = ODD[s]
                i = ODD_NO[s]
                if i == 0:
                    pe.wait_ge(s_z_even_ready, at("z_even_ready", l, NZ))
                    pe.wait_ge(s_z_odd_ready, at("z_odd_ready", l, NZ))
                elif s != ODD_ORDER[-1]:
                    pe.wait_ge(s_odd_job_read, at("odd_job_read", l, i))
                if what == "turn" and 0 < n < NB * NT - 1:
                    pe.wait_ge(s_outputs_lo_ready, at("outputs_lo_ready", l, n))
                if what == "iq":
                    for blk in range(2):
                        for t in range(NT):
                            ins = pe.transpose(ps[:, B_ODD, T * blk + P * t:T * blk + P * t + P],
                                               z1[:, t, C_IQ + P * blk:C_IQ + P * blk + P], ident[:])
                elif what == "ik":
                    pe.wait_ge(s_index_keys_copied, at("index_keys_copied", l, 1))
                    for t in range(NT):
                        pe.transpose(ps[:, B_ODD, P * t:P * t + P], ikd[:, t, :], ident[:])
                        ins = pe.transpose(ps[0:HD, B_ODD, T + P * t:T + P * t + P], z1[:, t, C_SK:C_SK + HD], ident[:])
                elif what == "cum":
                    pe.wait_ge(s_log_forgets_ready, at("log_forgets_ready", l, 1))
                    pe.matmul(ps[:, B_ODD, 0:H], tri[:, 0:P], fx[:, 0, :], start=True, stop=True)
                    pe.matmul(ps[:, B_ODD, H:2 * H], tri[:, P:T], fx[:, 0, :], start=True, stop=False)
                    ins = pe.matmul(ps[:, B_ODD, H:2 * H], tri[:, 0:P], fx[:, 1, :], start=False, stop=True)
                elif what == "index":
                    t = 0 if n < 2 else 1
                    hs = range(4 * n, 4 * n + 4) if t == 0 else range(2 * (n - 2), 2 * (n - 2) + 2)
                    keys = P * (t + 1)
                    for j, h in enumerate(hs):
                        ins = pe.matmul(ps[:, B_ODD, keys * j:keys * j + keys], iqt[:, h // 4, P * t:P * t + P],
                                        ikt[:, h % 4, 0:keys], start=True, stop=True)
                else:
                    b, t = divmod(n, NT)
                    pe.wait_ge(s_outputs_normed, at("outputs_normed", l, b + 1))
                    for k in range(4):
                        ins = pe.transpose(odd_psum(s)[:, P * k:P * k + P], o_tok[:, t, P * k:P * k + P], ident[:])
                ins.then_inc(s_odd_product, 1)

            def scores(l, hh):
                b, h = divmod(hh, H)
                bank, buf, d = B_S, hh % 2, HEAD_ROWS[b]
                pe.wait_ge(s_head_ready, at("head_ready", l, hh + 1))
                if hh > 0:
                    pe.wait_ge(s_probs_ready, at("probs_ready", l, hh))
                if hh == 2 * H:
                    pe.wait_ge(s_selection_ready, at("selection_ready", l, 1))
                q = qks[0:d, buf, 0, :]
                k = skt[:, :] if b == 2 else qks[0:d, buf, 1, :]
                pe.matmul(ps[:, bank, 0:P], q[:, 0:P], k[:, 0:P], start=True, stop=False)
                pe.matmul(ps[:, bank, 0:P], ident_b[:], selm[:, 0:P] if b == 2 else mask_b[:], start=False, stop=True)
                pe.matmul(ps[:, bank, P:3 * P], q[:, P:T], k[:, 0:T], start=True, stop=False)
                if b == 2:
                    ins = pe.matmul(ps[:, bank, P:3 * P], ident_b[:], selm[:, P:3 * P], start=False, stop=True)
                else:
                    ins = pe.matmul(ps[:, bank, T:3 * P], ident_b[:], mask_b[:], start=False, stop=True)
                ins.then_inc(s_scores_ready, 1)

            def turn_probs(l, hh):
                pe.wait_ge(s_probs_ready, at("probs_ready", l, hh + 1))
                if hh > 0:
                    pe.wait_ge(s_turned_probs_ready, at("turned_probs_ready", l, hh))
                for i in range(3):
                    ins = pe.transpose(ps[:, B_PT, P * i:P * i + P], prob[:, hh % 2, P * i:P * i + P], ident[:])
                ins.then_inc(s_probs_turned, 1)

            def values(l, hh):
                b, h = divmod(hh, H)
                pe.wait_ge(s_turned_probs_ready, at("turned_probs_ready", l, hh + 1))
                if hh == 0:
                    pe.wait_ge(s_z_even_ready, at("z_even_ready", l, NZ))
                    pe.wait_ge(s_z_odd_ready, at("z_odd_ready", l, NZ))
                elif h == 0:
                    pe.wait_ge(s_outputs_normed, at("outputs_normed", l, b))
                v = [v_tok[:, t, HD * h:HD * h + HD] if b == 0 else
                     z1[:, t, C_FV + HD * h:C_FV + HD * h + HD] if b == 1 else z1[:, t, C_SV:C_SV + HD]
                     for t in range(NT)]
                cols, buf = slice(HD * h, HD * h + HD), hh % 2
                pe.matmul(ps[:, B_O[0], cols], pts[:, buf, 0:P], v[0], start=True, stop=True)
                pe.matmul(ps[:, B_O[1], cols], pts[:, buf, P:T], v[0], start=True, stop=False)
                pe.matmul(ps[:, B_O[1], cols], pts[:, buf, T:3 * P], v[1], start=False, stop=True).then_inc(s_head_output, 1)

            def branch_panel(l, q, tiles=range(4)):
                n, c = divmod(q, 2)
                whi, wlo = panel(l, BR_AT + q, 4, 512)
                if c == 0:
                    pe.wait_ge(s_outputs_lo_ready, at("outputs_lo_ready", l, NT * (n + 1)))
                for jj in tiles:
                    u = 8 * n + 4 * c + jj
                    if u == 0:
                        pe.wait_ge(s_gate_ready, at("gate_ready", l, SLOTS))
                    if u == 2:
                        pe.wait_ge(s_head_ready, at("head_ready", l, SLOTS))
                    if u == KD:
                        pe.wait_ge(s_probs_ready, at("probs_ready", l, SLOTS))
                    if u == KD + 1:
                        pe.wait_ge(s_turned_probs_ready, at("turned_probs_ready", l, SLOTS))
                    before = [v for v in range(u) if B_PROJ[v] == B_PROJ[u]]
                    if before:
                        pe.wait_ge(s_proj_gated, at("proj_gated", l, before[-1] + 1))
                    dst = proj_psum(u)
                    for k in range(4):
                        cols = slice(P * jj, P * jj + P)
                        ins = product(dst, whi[:, k, cols], wlo[:, k, cols], ot_hi[:, 4 * n + k, :],
                                      ot_lo[:, 4 * n + k, :], k == 0, k == 3)
                    if jj < 3:
                        ins.then_inc(s_proj_product, 1)
                    else:
                        ins.then_inc(s_panel_used, 1)

            def ffn_up(l, f, slot, first):
                pe.wait_ge(s_weights_lo, at("weights_lo", l, UP_AT + f + 1))
                if not first:
                    pe.wait_ge(s_hidden_ready, at("hidden_ready", l, f - 1))
                whi, wlo = view(w_hi, slot, KD, 2 * P), view(w_lo, slot, KD, 2 * P)
                for i in range(2):
                    for k in range(KD):
                        if f == 0 and i == 0 and k == KD // 2:
                            pe.wait_ge(s_x_lo_ready, at("x_lo_ready", l, 8))
                        cols = slice(P * i, P * i + P)
                        ins = product(ps[:, slot, T * i:T * i + T], whi[:, k, cols], wlo[:, k, cols],
                                      xt_hi[:, k, :], xt_lo[:, k, :], k == 0, k == KD - 1)
                ins.then_inc(s_panel_used, 1)

            pe.wait_ge(s_const, N_CONST)
            with pe.Fori(0, DEPTH) as l:
                turn_x(l, 0)
                keep_clock_up(2, 8)
                pe.wait_ge(s_x_lo_ready, at("x_lo_ready", l, 3))
                z_panel(l, 0, 0)
                pe.wait_ge(s_vecs, 16 * N_VECS * (l + 1))
                pe.transpose(ps[:, 2, 0:P], vecs[:], ident[:]).then_inc(s_vectors_turned, 1)
                pe.wait_ge(s_x_lo_ready, at("x_lo_ready", l, 4))
                z_panel(l, 0, 1)
                pe.wait_ge(s_vectors_ready, at("vectors_ready", l, 1))
                z_panel(l, 1, 0)
                z_panel(l, 1, 1)
                latents(l)
                z_panel(l, 2, 0)
                z_panel(l, 2, 1)
                z_panel(l, 3, 0)
                mla_queries(l)
                z_panel(l, 3, 1)
                z_panel(l, 4, 0)
                mla_keys(l)
                z_panel(l, 4, 1)
                z_panel(l, 5, 0)
                z_panel(l, 5, 1)
                for s in range(LAST_SLOT + 1):
                    if s < SLOTS:
                        if s >= 2 * H:
                            head_operands_ready(l, s)
                        gate_tile(l, s)
                        if s < 2 * H:
                            head_operands_ready(l, s)
                        head_operands(l, s)
                    for job in odd_jobs(s):
                        odd_job(l, job)
                    if s == SLOTS:
                        branch_panel(l, 0, (0, 1))
                    if 0 <= s - LAG_S < SLOTS:
                        scores(l, s - LAG_S)
                    if 0 <= s - LAG_T < SLOTS:
                        turn_probs(l, s - LAG_T)
                    if 0 <= s - LAG_V < SLOTS:
                        values(l, s - LAG_V)
                    if 0 <= s - SLOTS < 4:
                        branch_panel(l, s - SLOTS, (2, 3) if s == SLOTS else range(4))
                branch_panel(l, 4)
                branch_panel(l, 5)
                for kh in range(2):
                    pe.wait_ge(s_merged_lo_ready, at("merged_lo_ready", l, 4 * kh + 4))
                    for t, ins in by_token(l, OUT_AT + kh, 4 * kh, 4, 512, (mg_hi, mg_lo), B_R[0], kh == 0, kh == 1):
                        if kh == 1 and t == 0:
                            ins.then_inc(s_residual_product, 1)
                    ins.then_inc(s_panel_used, 1)
                last_two_panels(l, OUT_AT + 2, (0, 4), (4, 4), (mg_hi, mg_lo), True)
                turn_x(l, 1)
                pe.wait_ge(s_x_lo_ready, at("x_lo_ready", l, 7))
                for f in range(FT):
                    ffn_up(l, f, (UP_AT + f) % 2, f < 2)
                ng = len(DOWN_K)
                for c in range(2):
                    for g in range(ng if c == 0 else ng - 2):
                        k0, nk = sum(DOWN_K[:g]), DOWN_K[g]
                        if c == 0:
                            pe.wait_ge(s_hidden_lo_ready, at("hidden_lo_ready", l, k0 + nk))
                        for t, ins in by_token(l, DOWN_AT + ng * c + g, k0, nk, 512, (ht_hi, ht_lo), B_R[c],
                                               g == 0, g == ng - 1):
                            if g == ng - 1 and t == 0:
                                ins.then_inc(s_residual_product, 1)
                        ins.then_inc(s_panel_used, 1)
                last_two_panels(l, NP - 2, (FT - sum(DOWN_K[-2:]), FT - DOWN_K[-1]), DOWN_K[-2:], (ht_hi, ht_lo), False)

        @block.scalar
        def _(act):
            def split_hi(l, p):
                act.wait_ge(loaded[p % RAW], loaded_count(l, p))
                if p >= 2:
                    act.wait_ge(s_panel_used, at("panel_used", l, p - 1))
                for n, cols in panel_extents(p):
                    ins = act.activation(w_hi[0:n, p % 2, cols], raw[0:n, p % RAW, cols], ACT.Copy)
                ins.then_inc(s_weights_hi, 1)

            def x_hi(l, j, t):
                for half in range(2):
                    act.wait_ge(s_x_turned, at("x_turned", l, 4 * j + 2 * t + half + 1))
                    dst, src = x_half(t, half)
                    act.activation(xt_hi[dst], src, ACT.Copy).then_inc(s_x_hi_ready, 1)

            def z_out(l, i):
                act.wait_ge(s_z_product, at("z_product", l, i + 1))
                act.activation(z1[:, 0, ZC * i:ZC * i + ZC], ps[:, B_Z[i][0], 0:ZC], ACT.Copy).then_inc(s_z_even_ready, 1)

            def gate(l, s):
                if s % 2 == 1:
                    act.wait_ge(s_panel_used, at("panel_used", l, GATE_AT + s // 2 + 1))
                else:
                    act.wait_ge(s_gate_product, at("gate_product", l, s // 2 + 1))
                act.activation(gates[:, s, :], ps[:, B_GATE[s % 2], 0:T], ACT.Tanh,
                                   scale=0.5, bias=bg2[:, s:s + 1]).then_inc(s_gate_ready, 1)

            def head_out(l, s):
                b = s // H
                d = HEAD_ROWS[b]
                act.wait_ge(s_head_turned, at("head_turned", l, s + 1))
                if s >= 2:
                    act.wait_ge(s_scores_ready, at("scores_ready", l, s - 1))
                if b < 2:
                    ins = act.activation(qks[0:d, s % 2, :, :], ps[0:d, B_QK, :].rearrange("p (a t) -> p a t", a=2),
                                         ACT.Copy)
                else:
                    ins = act.activation(qks[0:d, s % 2, 0, :], ps[0:d, B_QK, 0:T], ACT.Copy, scale=HD ** -0.5)
                ins.then_inc(s_head_ready, 1)

            def odd_out(l, s):
                what, n = ODD[s]
                act.wait_ge(s_odd_product, at("odd_product", l, ODD_NO[s] + 1))
                if what == "iq":
                    ins = act.activation(iqt[:], ps[:, B_ODD, :].rearrange("p (b t) -> p b t", b=2), ACT.Copy)
                elif what == "ik":
                    for j in range(4):
                        act.activation(ikt[:, j, :], ps[:, B_ODD, 0:T], ACT.Copy, scale=group[:, j:j + 1])
                    ins = act.activation(skt[:], ps[0:HD, B_ODD, T:2 * T], ACT.Copy)
                elif what == "cum":
                    cum = ps[:, B_ODD, 0:2 * H].rearrange("p (t h) -> p t h", t=NT)
                    act.wait_ge(s_decay_operands_ready, at("decay_operands_ready", l, 1))
                    act.activation(fq_aug[:, :, :, HD], cum, ACT.Copy)
                    ins = act.activation(fk_aug[:, :, :, HD + 1], cum, ACT.Copy, scale=-1.0)
                elif what == "index":
                    if n >= 2:
                        act.wait_ge(s_index_head_added, at("index_head_added", l, n - 1))
                    ins = act.activation(rel[:, n % 2, :], ps[:, B_ODD, :], ACT.Relu)
                else:
                    b, t = divmod(n, NT)
                    ins = act.activation(ot_hi[:, 4 * b:4 * b + 4, P * t:P * t + P],
                                         odd_psum(s).rearrange("p (k t) -> p k t", k=4), ACT.Copy)
                ins.then_inc(s_odd_job_read, 1)

            def softmax_exp(l, hh):
                b, h = divmod(hh, H)
                act.wait_ge(s_maxima_ready, at("maxima_ready", l, hh + 1))
                if hh >= 2:
                    act.wait_ge(s_probs_turned, at("probs_turned", l, hh - 1))
                for t in range(NT):
                    cols = SPAN[t]
                    src = ssc[:, cols] if b == 2 else ps[:, B_S, cols]
                    ins = act.activation(prob[:, hh % 2, cols], src, ACT.Exp, bias=negm[:, hh % 2, t:t + 1],
                                         accum_out=rsum[:, b, t, h:h + 1])
                ins.then_inc(s_probs_ready, 1)

            def merged_hi(l, j):
                act.wait_ge(s_merged_added, at("merged_added", l, (NB - 2) * KD + j + 1))
                act.activation(mg_hi[:, j, :], merged[:, j, :], ACT.Copy, scale=0.5).then_inc(s_merged_hi_ready, 1)

            def deviation(l, j, t):
                act.wait_ge(s_variances_ready, at("variances_ready", l, NT * j + t + 1))
                act.activation(dev[:, t:t + 1], mv[:, t, 1:2], ACT.Sqrt, bias=eps[:, 0:1]).then_inc(s_deviations_ready, 1)

            def norm_scale(l, j):
                act.wait_ge(s_centred, at("centred", l, j + 1))
                for half in range(2):
                    cols = slice(512 * half, 512 * half + 512)
                    act.activation(res[:, 0, cols], res[:, 0, cols], ACT.Copy, scale=rdev[:, 0:1]).then_inc(s_scaled, 1)

            def conv_first(l, f, buf):
                act.wait_ge(s_panel_used, at("panel_used", l, UP_AT + f + 1))
                act.activation(cv[:, buf, :], ps[:, buf, 0:T], ACT.Copy,
                                   scale=column(vec_t, V_CW + 2 * FT, f)).then_inc(s_conv_first_tap, 1)

            def gelu(l, f, buf, first):
                act.wait_ge(s_conv_ready, at("conv_ready", l, f + 1))
                if not first:
                    act.wait_ge(s_hidden_ready, at("hidden_ready", l, f - 1))
                act.activation(ge[:, buf, :], cv[:, buf, :], ACT.Gelu, bias=column(vec_t, V_CB, f)).then_inc(s_gelu_ready, 1)

            def hidden_hi(l, f, buf):
                act.wait_ge(s_hidden_ready, at("hidden_ready", l, f + 1))
                act.activation(tile_at(ht_hi, f), hf[:, buf, :], ACT.Copy).then_inc(s_hidden_hi_ready, 1)

            def load_vectors(l):
                one = bass.ds(l, 1)
                for dst, src in (
                    (vecs[V_CW:V_CB, :], conv_w[one].rearrange("a j (f n) -> (a j f) n", n=P)),
                    (vecs[V_CB:V_BG, :], conv_b[one].rearrange("a (f n) -> (a f) n", n=P)),
                    (vecs[V_BG:V_QN, :], b_gate[one].rearrange("a j (f n) -> (a j f) n", n=P)),
                    (vecs[V_QN:V_QN + 1, :], q_norm[one, 0:P]),
                    (vecs[V_QN + 1:V_QN + 2, 0:QR - P], q_norm[one, P:QR]),
                    (vecs[V_KN:V_END, :], kv_norm[one]),
                    (bfor[:], b_forget[one].rearrange("a h -> (a h)").partition_broadcast(P)),
                ):
                    act.dma_start(dst, src).then_inc(s_vecs, 16)

            def load_norm(l, g, b):
                one = bass.ds(l, 1)
                act.dma_start(ln_g[:], g[one].rearrange("a d -> (a d)").partition_broadcast(P)).then_inc(s_gb, 16)
                act.dma_start(ln_b[:], b[one].rearrange("a d -> (a d)").partition_broadcast(P)).then_inc(s_gb, 16)

            act.dma_start(pos_row[:], positions.partition_broadcast(P)).then_inc(s_in, 16)
            act.dma_start(pos_col[:], positions.rearrange("a (t p) -> p (a t)", p=P),
                          allow_slow_non_contiguous=True).then_inc(s_in, 16)
            act.wait_ge(s_setup, 1)
            act.wait_ge(s_x_in[0], 16)
            for i in range(2):
                act.activation(scratch[:, i:i + 1], eps[:, 0:1], ACT.Copy).then_inc(s_x_ready_0, 1)
            act.wait_ge(s_x_in[1], 16)
            for i in range(2, 4):
                act.activation(scratch[:, i:i + 1], eps[:, 0:1], ACT.Copy).then_inc(s_x_ready_1, 1)
            with act.Fori(0, DEPTH) as l:
                x_hi(l, 0, 0)
                split_hi(l, 0)
                x_hi(l, 0, 1)
                load_vectors(l)
                for p in range(GATE_AT):
                    split_hi(l, p + 1)
                    if p == 0:
                        act.wait_ge(s_vectors_turned, at("vectors_turned", l, 1))
                        act.activation(vec_t[:], ps[:, 2, 0:P], ACT.Copy).then_inc(s_vectors_ready, 1)
                    if p in Z_LAST:
                        z_out(l, Z_LAST.index(p))
                    if p == 2:
                        act.wait_ge(s_latent_squares, at("latent_squares", l, 1))
                        act.activation(small[:, 4:6], small[:, 0:2], ACT.Sqrt, scale=1.0 / QR, bias=eps[:, 1:2])
                        act.activation(small[:, 6:8], small[:, 2:4], ACT.Sqrt, scale=1.0 / KVR,
                                           bias=eps[:, 1:2]).then_inc(s_latent_rms, 1)
                    if p == 4:
                        act.wait_ge(s_latents_scaled, at("latents_scaled", l, 1))
                        act.activation(c_hi[:, 0:2, :], c_f[:, 0:2, :], ACT.Copy)
                        act.activation(c_hi[0:QR - P, 2, :], c_f[0:QR - P, 2, :], ACT.Copy).then_inc(s_latents_hi, 1)
                    if p == UQ_AT:
                        act.wait_ge(s_setup, 2)
                        act.activation(sin[:], ang[:], ACT.Sin)
                        act.activation(cos[:], angc[:], ACT.Sin).then_inc(s_rotations_ready, 1)
                        for t in range(NT):
                            if t == 1:
                                act.wait_ge(s_panel_used, at("panel_used", l, UQ_AT + 1))
                            else:
                                act.wait_ge(s_mla_q_product, at("mla_q_product", l, 1))
                            act.activation(q_tok[:, t, :].rearrange("p (c n) -> p c n", c=2),
                                               ps[:, 4 + 2 * t:6 + 2 * t, 0:384], ACT.Copy, scale=QK ** -0.5).then_inc(s_mla_q_ready, 1)
                    if p == UKV_AT:
                        for c in range(2):
                            act.wait_ge(s_mla_kv_product, at("mla_kv_product", l, 2 * c + 1))
                            kd, ks, vd, vs = keys_values(c, 0)
                            act.activation(kd, ks, ACT.Copy)
                            act.activation(vd, vs, ACT.Copy).then_inc(s_mla_kv_even_ready, 1)
                    if p == Z_AT[4][1] + 1:
                        act.wait_ge(s_forget_logits_ready, at("forget_logits_ready", l, 1))
                        act.activation(fe[:], fe[:], ACT.Exp)
                        act.drain()
                        act.activation(fl[:], fe[:], ACT.Ln, bias=1.0).then_inc(s_forget_logs_ready, 1)
                act.wait_ge(s_gate_bias_ready, at("gate_bias_ready", l, 1))
                for s in range(LAST_SLOT + 1):
                    if s % 2 == 0 and s < SLOTS:
                        split_hi(l, GATE_AT + s // 2 + 1)
                    if s < SLOTS:
                        gate(l, s)
                        head_out(l, s)
                    for job in odd_jobs(s):
                        odd_out(l, job)
                    if s == SLOTS:
                        split_hi(l, BR_AT + 1)
                    if 0 <= s - LAG_S < SLOTS:
                        softmax_exp(l, s - LAG_S)
                    if 0 < s - SLOTS < 4:
                        split_hi(l, BR_AT + s - SLOTS + 1)
                split_hi(l, BR_AT + 5)
                merged_hi(l, 0)
                merged_hi(l, 1)
                split_hi(l, OUT_AT)
                merged_hi(l, 2)
                merged_hi(l, 3)
                for q in range(3):
                    split_hi(l, OUT_AT + q + 1)
                    if q == 0:
                        for j in range(KD // 2, KD):
                            merged_hi(l, j)
                    if q == 1:
                        act.wait_ge(s_merged_lo_ready, at("merged_lo_ready", l, KD))
                        load_norm(l, ln1_g, ln1_b)
                act.activation(scratch[:, 0:1], eps[:, 0:1], ACT.Sqrt)
                split_hi(l, UP_AT)
                deviation(l, 0, 0)
                norm_scale(l, 0)
                deviation(l, 0, 1)
                split_hi(l, UP_AT + 1)
                x_hi(l, 1, 0)
                x_hi(l, 1, 1)
                for f in range(FT):
                    if f > 0:
                        split_hi(l, UP_AT + f + 1)
                    if f >= 1:
                        gelu(l, f - 1, (f - 1) % 2, f < 3)
                    if f >= 2:
                        hidden_hi(l, f - 2, f % 2)
                    conv_first(l, f, f % 2)
                for p in range(DOWN_AT, NP):
                    if p < NP - 1:
                        split_hi(l, p + 1)
                    if p == DOWN_AT:
                        gelu(l, FT - 1, (FT - 1) % 2, False)
                        hidden_hi(l, FT - 2, FT % 2)
                        hidden_hi(l, FT - 1, (FT - 1) % 2)
                    if p == DOWN_AT + 1:
                        load_norm(l, ln2_g, ln2_b)
                deviation(l, 1, 0)
                norm_scale(l, 1)
                deviation(l, 1, 1)

        @block.vector
        def _(dve):
            def split_lo(l, p):
                dve.wait_ge(s_weights_hi, at("weights_hi", l, p + 1))
                for n, cols in panel_extents(p):
                    ins = dve.tensor_tensor(w_lo[0:n, p % 2, cols], raw[0:n, p % RAW, cols],
                                            w_hi[0:n, p % 2, cols].bitcast(F32), ALU.subtract)
                ins.then_inc(s_weights_lo, 1)

            def x_lo(l, j, t, half):
                dve.wait_ge(s_x_hi_ready, at("x_hi_ready", l, 4 * j + 2 * t + half + 1))
                dst, src = x_half(t, half)
                dve.tensor_tensor(xt_lo[dst], src, xt_hi[dst].bitcast(F32), ALU.subtract).then_inc(s_x_lo_ready, 1)

            def z_out(l, i):
                dve.wait_ge(s_panel_used, at("panel_used", l, Z_LAST[i] + 1))
                dve.tensor_copy(z1[:, 1, ZC * i:ZC * i + ZC], ps[:, B_Z[i][1], 0:ZC]).then_inc(s_z_odd_ready, 1)

            def rms_sums(l):
                dve.drain()
                dve.wait_ge(s_z_even_ready, at("z_even_ready", l, 1))
                for t in range(NT):
                    for i, (c, n) in enumerate(((C_CQ, QR), (C_CKV, KVR))):
                        z = z1[:, t, c:c + n]
                        ins = dve.tensor_tensor_reduce(cn[:, t, c:c + n], z, z, 1.0, 0.0, ALU.mult, ALU.add,
                                                       accum_out=small[:, 2 * i + t:2 * i + t + 1])
                ins.then_inc(s_latent_squares, 1)

            def rms_scale(l):
                dve.wait_ge(s_latent_rms, at("latent_rms", l, 1))
                dve.reciprocal(small[:, 8:12], small[:, 4:8])
                dve.drain()
                for t in range(NT):
                    for i, (c, n) in enumerate(((C_CQ, QR), (C_CKV, KVR))):
                        ins = dve.tensor_scalar(cn[:, t, c:c + n], z1[:, t, c:c + n],
                                                small[:, 8 + 2 * i + t:9 + 2 * i + t], None, ALU.mult)
                ins.then_inc(s_latents_normed, 1)

            def latent_gain(l):
                dve.wait_ge(s_latents_turned, at("latents_turned", l, 1))
                dve.tensor_scalar(c_f[:, 0, :], ps[:, B_LAT[0], 0:T], vec_t[:, V_QN:V_QN + 1], None, ALU.mult)
                dve.tensor_scalar(c_f[:, 1, :], ps[:, B_LAT[0], T:2 * T], vec_t[:, V_KN:V_KN + 1], None, ALU.mult)
                r = QR - P
                dve.tensor_scalar(c_f[0:r, 2, :], ps[0:r, B_LAT[1], 0:T], vec_t[0:r, V_QN + 1:V_QN + 2], None,
                                      ALU.mult).then_inc(s_latents_scaled, 1)

            def latent_lo(l):
                dve.wait_ge(s_latents_hi, at("latents_hi", l, 1))
                dve.tensor_tensor(c_lo[:, 0:2, :], c_f[:, 0:2, :], c_hi[:, 0:2, :].bitcast(F32), ALU.subtract)
                r = QR - P
                dve.tensor_tensor(c_lo[0:r, 2, :], c_f[0:r, 2, :], c_hi[0:r, 2, :].bitcast(F32),
                                      ALU.subtract).then_inc(s_latents_lo, 1)

            def rotate(first, second, c, s, tmp, out1, out2):
                for i, (a, b) in enumerate(((first, c), (second, s), (first, s), (second, c))):
                    dve.tensor_tensor(tmp[i], a, b, ALU.mult)
                dve.drain()
                dve.tensor_tensor(out1, tmp[0], tmp[1], ALU.subtract)
                return dve.tensor_tensor(out2, tmp[2], tmp[3], ALU.add)

            def rotate_queries(l):
                dve.wait_ge(s_rotations_ready, at("rotations_ready", l, 1))
                dve.wait_ge(s_mla_q_ready, at("mla_q_ready", l, NT))
                qt = q_tok[:].rearrange("p t (h n) -> p t h n", n=QK)
                q1, q2 = qt[:, :, :, HD:HD + HALF], qt[:, :, :, HD + HALF:QK]
                c, s = (w[:, :, None, :].broadcast_to([P, NT, H, HALF]) for w in (cos, sin))
                rotate(q1, q2, c, s, [rot[:, i] for i in range(4)], q1, q2)

            def rotate_keys(l):
                k1, k2 = z1[:, :, C_KR:C_KR + HALF], z1[:, :, C_KR + HALF:C_KR + ROPE]
                rotate(k1, k2, cos[:], sin[:], [krot[:, i] for i in range(4)], kr[:, :, 0:HALF], kr[:, :, HALF:])
                dve.drain()
                kt = k_tok[:].rearrange("p t (h n) -> p t h n", n=QK)
                dve.tensor_copy(kt[:, :, :, HD:QK],
                                kr[:, :, None, :].broadcast_to([P, NT, H, ROPE])).then_inc(s_rotated, 1)

            def forget_logits(l):
                dve.drain()
                dve.wait_ge(s_z_even_ready, at("z_even_ready", l, 5))
                dve.tensor_tensor(fx[:], z1[:, :, C_FL:C_FL + H], bfor[:, None, :].broadcast_to([P, NT, H]), ALU.add)
                dve.drain()
                dve.scalar_tensor_tensor(fe[:], fx[:], -1.0, fx[:], ALU.mult, ALU.min).then_inc(s_forget_logits_ready, 1)

            def log_forget(l):
                dve.wait_ge(s_forget_logs_ready, at("forget_logs_ready", l, 1))
                dve.scalar_tensor_tensor(fx[:], fx[:], 0.0, fl[:], ALU.min, ALU.subtract).then_inc(s_log_forgets_ready, 1)

            def index_keys(l):
                dve.drain()
                dve.wait_ge(s_z_even_ready, at("z_even_ready", l, NZ))
                for t in range(NT):
                    ins = dve.tensor_copy(ikd[:, t, :].rearrange("p (j n) -> p j n", j=4),
                                          z1[:, t, C_IK:C_IK + IDIM][:, None, :].broadcast_to([P, 4, IDIM]))
                ins.then_inc(s_index_keys_copied, 1)

            def index_scores(l, n):
                t = 0 if n < 2 else 1
                hs = range(4 * n, 4 * n + 4) if t == 0 else range(2 * (n - 2), 2 * (n - 2) + 2)
                keys = P * (t + 1)
                dve.drain()
                dve.wait_ge(s_odd_job_read, at("odd_job_read", l, 3 + n + 1))
                for j, h in enumerate(hs):
                    w = z1[:, t, C_IW + h:C_IW + h + 1]
                    r = rel[:, n % 2, keys * j:keys * j + keys]
                    if h == 0:
                        ins = dve.tensor_scalar(ix[:, SPAN[t]], r, w, None, ALU.mult)
                    else:
                        if j:
                            dve.drain()
                        ins = dve.scalar_tensor_tensor(ix[:, SPAN[t]], r, w, ix[:, SPAN[t]], ALU.mult, ALU.add)
                ins.then_inc(s_index_head_added, 1)

            def take_eight(t):
                dve.max(top8[:], ixw[:, SPAN[t]])
                dve.drain()
                dve.match_replace(ixw[:, SPAN[t]], top8[:], ixw[:, SPAN[t]], TAKEN)
                dve.drain()

            def selection(l):
                dve.tensor_scalar(selm[:], ixw[:], (LOWEST + TAKEN) / 2, MASKED, ALU.is_gt, ALU.mult)
                dve.drain()
                dve.tensor_tensor(selm[:, 0:P], selm[:, 0:P], mask_b[:], ALU.add)
                dve.tensor_tensor(selm[:, T:3 * P], selm[:, T:3 * P], mask_b[:], ALU.add).then_inc(s_selection_ready, 1)

            def row_max(l, hh):
                b, h = divmod(hh, H)
                dve.wait_ge(s_scores_ready, at("scores_ready", l, hh + 1))
                if hh >= 2:
                    dve.wait_ge(s_probs_ready, at("probs_ready", l, hh - 1 if b < 2 else hh))
                for t in range(NT):
                    src = ps[:, B_S, SPAN[t]]
                    if b == 2:
                        dve.scalar_tensor_tensor(ssc[:, SPAN[t]], dist[:, t, 0:P * (t + 1)], -(2.0 ** -(8 * (h + 1) / H)),
                                                 src, ALU.mult, ALU.add)
                if b == 2:
                    dve.drain()
                for t in range(NT):
                    src = ssc[:, SPAN[t]] if b == 2 else ps[:, B_S, SPAN[t]]
                    ins = dve.tensor_reduce(negm[:, hh % 2, t:t + 1], src, AX.X, ALU.max, negate=True)
                ins.then_inc(s_maxima_ready, 1)

            def probs_out(l, hh):
                dve.wait_ge(s_probs_turned, at("probs_turned", l, hh + 1))
                if hh >= 2:
                    dve.wait_ge(s_head_output, at("head_output", l, hh - 1))
                dve.tensor_copy(pts[:, hh % 2, :], ps[:, B_PT, 0:3 * P]).then_inc(s_turned_probs_ready, 1)

            def normalise(l, b):
                dve.wait_ge(s_head_output, at("head_output", l, H * (b + 1)))
                if b:
                    dve.wait_ge(s_odd_product, at("odd_product", l, ODD_NO[H * b + LAG_V + 2] + 1))
                dve.reciprocal(rinv[:], rsum[:, b])
                dve.drain()
                for t in range(NT):
                    ins = dve.tensor_tensor(o_tok[:, t, :].rearrange("p (h n) -> p h n", h=H),
                                            ps[:, B_O[t], :].rearrange("p (h n) -> p h n", h=H),
                                            rinv[:, t, :][:, :, None].broadcast_to([P, H, HD]), ALU.mult)
                ins.then_inc(s_outputs_normed, 1)

            def turned_lo(l, s):
                b, t = divmod(ODD[s][1], NT)
                dve.wait_ge(s_odd_job_read, at("odd_job_read", l, ODD_NO[s] + 1))
                dst = (slice(None), slice(4 * b, 4 * b + 4), slice(P * t, P * t + P))
                dve.tensor_tensor(ot_lo[dst], odd_psum(s).rearrange("p (k t) -> p k t", k=4),
                                      ot_hi[dst].bitcast(F32), ALU.subtract).then_inc(s_outputs_lo_ready, 1)

            def merge(l, q, tiles=range(4)):
                n, c = divmod(q, 2)
                if q == 0 and 0 in tiles:
                    dve.wait_ge(s_gate_ready, at("gate_ready", l, SLOTS))
                for jj in tiles:
                    u = KD * n + 4 * c + jj
                    if jj == 3:
                        dve.wait_ge(s_panel_used, at("panel_used", l, BR_AT + q + 1))
                    else:
                        dve.wait_ge(s_proj_product, at("proj_product", l, 3 * q + jj + 1))
                    if u >= KD + NGATED:
                        dve.wait_ge(s_merged_added, at("merged_added", l, u - KD - NGATED + 1))
                    dst = merged[:, u, :] if n == 0 else gated[:, u % NGATED, :]
                    dve.scalar_tensor_tensor(dst, gates[:, u, :], 1.0, proj_psum(u), ALU.add,
                                             ALU.mult).then_inc(s_proj_gated, 1)

            def merged_lo(l, j):
                dve.wait_ge(s_merged_hi_ready, at("merged_hi_ready", l, j + 1))
                dve.scalar_tensor_tensor(mg_lo[:, j, :], merged[:, j, :], 0.5, mg_hi[:, j, :].bitcast(F32),
                                             ALU.mult, ALU.subtract).then_inc(s_merged_lo_ready, 1)

            def residual(l, j, c, t):
                cols = slice(512 * c, 512 * c + 512)
                dve.drain()
                if t == 0:
                    dve.wait_ge(s_residual_product, at("residual_product", l, 2 * j + c + 1))
                else:
                    p = DOWN_AT + len(DOWN_K) * (c + 1) - 1 if j else OUT_AT + 2 * c + 1
                    dve.wait_ge(s_panel_used, at("panel_used", l, p + 1))
                dve.scalar_tensor_tensor(res[:, t, cols], x_tok[:, t, cols], ALPHA, ps[:, B_R[c][t], :],
                                         ALU.mult, ALU.add)
                dve.drain()
                dve.bn_stats(stats[:, t, c, :], res[:, t, cols])

            def norm(l, j):
                for t in range(NT):
                    residual(l, j, 1, t)
                    dve.drain()
                    dve.bn_aggr(mv[:, t, :], stats[:, t, :, :]).then_inc(s_variances_ready, 1)
                    dve.drain()
                    dve.wait_ge(s_gb, 16 * (4 * l + 2 * j + 2))
                    for half in range(2):
                        cols = slice(512 * half, 512 * half + 512)
                        ins = dve.scalar_tensor_tensor(res[:, t, cols], res[:, t, cols], mv[:, t, 0:1], ln_g[:, cols],
                                                       ALU.subtract, ALU.mult)
                        if half == 0:
                            dve.wait_ge(s_deviations_ready, at("deviations_ready", l, NT * j + t + 1))
                            dve.reciprocal(rdev[:, t:t + 1], dev[:, t:t + 1])
                        if t == 0:
                            if half == 1:
                                ins.then_inc(s_centred, 1)
                            continue
                        dve.drain()
                        dve.scalar_tensor_tensor(x_tok[:, t, cols], res[:, t, cols], rdev[:, t:t + 1], ln_b[:, cols],
                                                 ALU.mult, ALU.add).then_inc(s_x_ready_1, 1)

            def conv_rest(l, f, buf):
                dve.wait_ge(s_conv_first_tap, at("conv_first_tap", l, f + 1))
                dve.scalar_tensor_tensor(cv[:, buf, 1:T], ps[:, buf, 0:T - 1], column(vec_t, V_CW + FT, f),
                                         cv[:, buf, 1:T], ALU.mult, ALU.add)
                dve.drain()
                dve.scalar_tensor_tensor(cv[:, buf, 2:T], ps[:, buf, 0:T - 2], column(vec_t, V_CW, f),
                                             cv[:, buf, 2:T], ALU.mult, ALU.add).then_inc(s_conv_ready, 1)

            def hidden(l, f, buf, first):
                dve.wait_ge(s_gelu_ready, at("gelu_ready", l, f + 1))
                if not first:
                    dve.wait_ge(s_hidden_hi_ready, at("hidden_hi_ready", l, f - 1))
                dve.tensor_tensor(hf[:, buf, :], ge[:, buf, :], ps[:, buf, T:2 * T], ALU.mult).then_inc(s_hidden_ready, 1)

            def hidden_lo(l, f, buf):
                dve.wait_ge(s_hidden_hi_ready, at("hidden_hi_ready", l, f + 1))
                dve.tensor_tensor(tile_at(ht_lo, f), hf[:, buf, :], tile_at(ht_hi, f).bitcast(F32),
                                      ALU.subtract).then_inc(s_hidden_lo_ready, 1)

            dve.memset(eps[:, 0:1], LN_EPS)
            dve.memset(eps[:, 1:2], RMS_EPS)
            dve.memset(group[:], 0.0)
            dve.memset(vecs[:], 0.0)
            dve.drain()
            for j in range(4):
                dve.memset(group[IDIM * j:IDIM * j + IDIM, j:j + 1], 1.0).then_inc(s_const, 1)
            for i in range(RAW):
                dve.memset(mv[:, i // 2, i % 2:i % 2 + 1], 0.0).then_inc(s_weights_lo, 1)
            dve.memset(freq[:, 0:1], float(inv_freq[0])).then_inc(s_setup, 1)
            for j in range(1, HALF):
                dve.memset(freq[:, j:j + 1], float(inv_freq[j]))
            dve.wait_ge(s_in, 32)
            dve.tensor_copy(pos_f[:], pos_row[:])
            dve.tensor_copy(pos_c[:], pos_col[:])
            dve.drain()
            for t in range(NT):
                dve.tensor_scalar(dist[:, t, :], pos_f[:], pos_c[:, t:t + 1], None, ALU.subtract)
                dve.tensor_scalar(ang[:, t, :], freq[:], pos_c[:, t:t + 1], None, ALU.mult)
            dve.drain()
            dve.scalar_tensor_tensor(dist[:], dist[:], -1.0, dist[:], ALU.mult, ALU.max)
            dve.tensor_scalar(turns[:], ang[:], 1.0 / (2 * np.pi), ROUND, ALU.mult, ALU.add)
            dve.drain()
            dve.tensor_scalar(turns[:], turns[:], -ROUND, None, ALU.add)
            dve.drain()
            for part in TWO_PI:
                dve.scalar_tensor_tensor(ang[:], turns[:], -part, ang[:], ALU.mult, ALU.add)
                dve.drain()
            dve.tensor_scalar(angc[:], ang[:], np.pi / 2, None, ALU.add)
            dve.drain()
            dve.tensor_scalar(turns[:], angc[:], np.pi, -2 * np.pi, ALU.is_gt, ALU.mult)
            dve.drain()
            dve.tensor_tensor(angc[:], angc[:], turns[:], ALU.add)
            dve.drain()
            dve.tensor_scalar(ang[:], ang[:], PI_BELOW, -PI_BELOW, ALU.min, ALU.max)
            dve.tensor_scalar(angc[:], angc[:], PI_BELOW, -PI_BELOW, ALU.min, ALU.max).then_inc(s_setup, 1)
            dve.wait_ge(s_const, N_CONST)
            with dve.Fori(0, DEPTH) as l:
                x_lo(l, 0, 0, 0)
                x_lo(l, 0, 0, 1)
                x_lo(l, 0, 1, 0)
                for part, cols in enumerate(FIRST_COLS[1:]):
                    dve.wait_ge(s_weights_hi, at("weights_hi", l, 1))
                    if part == 1:
                        dve.wait_ge(s_first_half_split, at("first_half_split", l, 1))
                    ins = dve.tensor_tensor(w_lo[:, 0, cols], raw[:, 0, cols], w_hi[:, 0, cols].bitcast(F32), ALU.subtract)
                ins.then_inc(s_weights_lo, 1)
                x_lo(l, 0, 1, 1)
                for p in range(GATE_AT):
                    split_lo(l, p + 1)
                    if p == UKV_AT + 1:
                        rotate_queries(l)
                    if p in Z_LAST:
                        z_out(l, Z_LAST.index(p))
                    if p == 0:
                        dve.wait_ge(s_vectors_ready, at("vectors_ready", l, 1))
                        dve.tensor_scalar(bg2[:], vec_t[:, V_BG:V_BG + NB * KD], 0.5, None,
                                          ALU.mult).then_inc(s_gate_bias_ready, 1)
                    if p == 1:
                        rms_sums(l)
                    if p == 2:
                        rms_scale(l)
                    if p == 4:
                        latent_gain(l)
                        latent_lo(l)
                    if p == UKV_AT:
                        for c in range(2):
                            if c == 0:
                                dve.wait_ge(s_mla_kv_product, at("mla_kv_product", l, 2))
                            else:
                                dve.wait_ge(s_panel_used, at("panel_used", l, p + 1))
                            kd, ks, vd, vs = keys_values(c, 1)
                            dve.tensor_copy(kd, ks)
                            dve.tensor_copy(vd, vs).then_inc(s_mla_kv_odd_ready, 1)
                    if p == Z_AT[4][1]:
                        forget_logits(l)
                    if p == Z_AT[4][1] + 1:
                        log_forget(l)
                        rotate_keys(l)
                index_keys(l)
                for s in range(LAST_SLOT + 1):
                    if s % 2 == 0 and s < SLOTS:
                        split_lo(l, GATE_AT + s // 2 + 1)
                    if s == 6:
                        dve.wait_ge(s_index_masked, at("index_masked", l, 1))
                    if s == 10:
                        dve.wait_ge(s_index_masked, at("index_masked", l, 2))
                    for job in odd_jobs(s):
                        if ODD[job][0] == "turn":
                            turned_lo(l, job)
                    if s == SLOTS:
                        merge(l, 0, (0, 1))
                    if 0 <= s - LAG_S < SLOTS:
                        row_max(l, s - LAG_S)
                    if 0 <= s - LAG_T < SLOTS:
                        probs_out(l, s - LAG_T)
                    if s - 4 in range(6):
                        index_scores(l, s - 4)
                    if 6 <= s < 14:
                        for _ in range(TOPK // 8 // 4):
                            take_eight(0 if s < 10 else 1)
                    if s == 14:
                        selection(l)
                    if s >= H + 2 and (s - H - 2) % H == 0:
                        normalise(l, (s - H - 2) // H)
                    if 0 <= s - SLOTS < 4:
                        split_lo(l, BR_AT + s - SLOTS + 1)
                        merge(l, s - SLOTS, (2, 3) if s == SLOTS else range(4))
                split_lo(l, BR_AT + 5)
                merge(l, 4)
                merged_lo(l, 0)
                merged_lo(l, 1)
                merge(l, 5, (0, 1))
                split_lo(l, OUT_AT)
                merged_lo(l, 2)
                merged_lo(l, 3)
                merge(l, 5, (2, 3))
                for q in range(4):
                    if q < 3:
                        split_lo(l, OUT_AT + q + 1)
                    if q == 0:
                        for j in range(KD // 2, KD):
                            merged_lo(l, j)
                    if q == 2:
                        residual(l, 0, 0, 0)
                        residual(l, 0, 0, 1)
                norm(l, 0)
                for t in range(NT):
                    for half in range(2):
                        x_lo(l, 1, t, half)
                dve.wait_ge(s_weights_lo, at("weights_lo", l, UP_AT + 1))
                for f in range(FT):
                    split_lo(l, UP_AT + f + 1)
                    if f >= 1:
                        hidden(l, f - 1, (f - 1) % 2, f < 3)
                    if f >= 2:
                        hidden_lo(l, f - 2, f % 2)
                    conv_rest(l, f, f % 2)
                for p in range(DOWN_AT, NP):
                    if p < NP - 1:
                        split_lo(l, p + 1)
                    if p == DOWN_AT:
                        hidden(l, FT - 1, (FT - 1) % 2, False)
                        hidden_lo(l, FT - 2, FT % 2)
                        hidden_lo(l, FT - 1, (FT - 1) % 2)
                    if p == DOWN_AT + len(DOWN_K) - 1:
                        residual(l, 1, 0, 0)
                        residual(l, 1, 0, 1)
                norm(l, 1)

        @block.gpsimd
        def _(pool):
            pool.memset(ident[:], 0.0)
            pool.memset(mask_b[:], 0.0)
            pool.memset(tri[:], 1.0).then_inc(s_pool, 1)
            pool.wait_ge(s_pool, 1)
            pool.affine_select(out=ident[:], in_=ident[:], compare_op=ALU.not_equal, fill=1.0, base=0,
                               pattern=[[-1, P]], channel_multiplier=1).then_inc(s_pool, 1)
            pool.affine_select(out=mask_b[:], in_=mask_b[:], compare_op=ALU.is_ge, fill=MASKED, base=0,
                               pattern=[[-1, P]], channel_multiplier=1).then_inc(s_const, 1)
            pool.affine_select(out=tri[:, 0:P], in_=tri[:, 0:P], compare_op=ALU.is_ge, fill=0.0, base=0,
                               pattern=[[1, P]], channel_multiplier=-1).then_inc(s_const, 1)
            pool.wait_ge(s_pool, 2)
            pool.tensor_copy(ident_b[:], ident[:]).then_inc(s_const, 1)
            def take_wait():
                pool.tensor_tensor(waited[:], group[:, 0:1], group[:, 0:1], ALU.mult)

            def split_lo(p, cols):
                return pool.tensor_tensor(w_lo[:, p % 2, cols], raw[:, p % RAW, cols],
                                          w_hi[:, p % 2, cols].bitcast(F32), ALU.subtract)

            def norm_bias(l, j):
                for half in range(2):
                    cols = slice(512 * half, 512 * half + 512)
                    pool.wait_ge(s_scaled, at("scaled", l, 2 * j + half + 1))
                    pool.tensor_tensor(x_tok[:, 0, cols], res[:, 0, cols], ln_b[:, cols], ALU.add).then_inc(s_x_ready_0, 1)

            pool.wait_ge(s_const, N_CONST)
            pool.wait_ge(s_x_ready_0, 2)
            pool.wait_ge(s_weights_lo, RAW)
            with pool.Fori(0, DEPTH) as l:
                pool.wait_ge(s_weights_hi, at("weights_hi", l, 1))
                split_lo(0, FIRST_COLS[0]).then_inc(s_first_half_split, 1)
                pool.wait_ge(s_z_even_ready, at("z_even_ready", l, 3))
                pool.wait_ge(s_z_odd_ready, at("z_odd_ready", l, 3))
                take_wait()
                for t in range(NT):
                    for dst, c, scale in ((fq_aug, C_FQ, HD ** -0.5), (fk_aug, C_FK, 1.0)):
                        pool.tensor_scalar(dst[:, t, :, 0:HD], z1[:, t, c:c + H * HD].rearrange("p (h n) -> p h n", h=H),
                                           scale, None, ALU.mult)
                pool.memset(fq_aug[:, :, :, HD + 1], 1.0)
                pool.memset(fk_aug[:, :, :, HD], 1.0).then_inc(s_decay_operands_ready, 1)
                pool.wait_ge(s_index_head_added, at("index_head_added", l, 2))
                take_wait()
                pool.affine_select(out=ixw[:, SPAN[0]], in_=ix[:, SPAN[0]], compare_op=ALU.is_ge, fill=LOWEST,
                                       base=0, pattern=[[-1, P]], channel_multiplier=1).then_inc(s_index_masked, 1)
                pool.wait_ge(s_index_head_added, at("index_head_added", l, 6))
                take_wait()
                pool.affine_select(out=ixw[:, SPAN[1]], in_=ix[:, SPAN[1]], compare_op=ALU.is_ge, fill=LOWEST,
                                       base=P, pattern=[[-1, T]], channel_multiplier=1).then_inc(s_index_masked, 1)
                for u in range(KD, NB * KD):
                    pool.wait_ge(s_proj_gated, at("proj_gated", l, u + 1))
                    if u >= 2 * KD:
                        pool.wait_ge(s_merged_added, at("merged_added", l, u - 2 * KD + 1))
                    pool.tensor_tensor(merged[:, u % KD, :], merged[:, u % KD, :], gated[:, u % NGATED, :],
                                       ALU.add).then_inc(s_merged_added, 1)
                pool.wait_ge(s_weights_hi, at("weights_hi", l, UP_AT + 1))
                split_lo(UP_AT, slice(0, PANEL * 3 // 8))
                norm_bias(l, 0)
                split_lo(UP_AT, slice(PANEL * 3 // 8, PANEL)).then_inc(s_weights_lo, 1)
                norm_bias(l, 1)

    return nc


_ARGS = ["x", "positions", "w_in", "b_gate", "b_forget", "mla_q_norm", "mla_kv_norm", "mla_w_uq", "mla_w_ukv",
         "w_branch", "w_out", "ln1_g", "ln1_b", "ffn_w_up", "ffn_conv_w", "ffn_conv_b", "ffn_w_down", "ln2_g", "ln2_b"]


def kernel(**inputs):
    import concourse.bacc as bacc
    from concourse.bass_utils import run_bass_kernel_spmd

    nc = bacc.Bacc("TRN2", target_bir_lowering=False, num_devices=1)
    arrays = {n: np.ascontiguousarray(inputs[n]) for n in _ARGS}
    args = [nc.dram_tensor(n, a.shape, mybir.dt.from_np(a.dtype), kind="ExternalInput").ap() for n, a in arrays.items()]
    out = nc.dram_tensor("out", arrays["x"].shape, F32, kind="ExternalOutput").ap()
    build_program(nc, *args, out)
    return run_bass_kernel_spmd(nc, [arrays], core_ids=[0]).results[0]["out"]
```
